# Optimizing a Trainium2 kernel written in Bass

```python
import math
import jax, jax.numpy as jnp
from jax import lax
import numpy as np

D_MODEL = 2048
BATCH = 1
SEQ = 256
DEPTH = 1

CHUNK = 64
QBLOCK = 128
EPS = 1e-6

MLA_HEADS = 8
MLA_NOPE = 128
MLA_ROPE = 64
MLA_V = 128
MLA_QK = MLA_NOPE + MLA_ROPE
Q_LORA = 512
KV_LORA = 256
ROPE_THETA = 10000.0

DSA_HEADS = 8
DSA_HD = 128
IDX_HEADS = 16
IDX_HD = 64
DSA_TOPK = 256

REL_BUCKETS = 32
REL_MAX_DIST = 128

PEER_HEADS = 8
PEER_NKEYS = 128
PEER_EXPERTS = PEER_NKEYS * PEER_NKEYS
PEER_DKEY = 256
PEER_TOPK = 16

MIX_WIDTH = MLA_HEADS * MLA_V + DSA_HEADS * DSA_HD
IN_SPLITS = (Q_LORA, KV_LORA, MLA_ROPE,
             DSA_HEADS * DSA_HD, DSA_HEADS * DSA_HD, DSA_HEADS * DSA_HD,
             IDX_HEADS * IDX_HD, IDX_HD, IDX_HEADS)
IN_WIDTH = sum(IN_SPLITS)
IN_OFFSETS = tuple(int(o) for o in np.cumsum(IN_SPLITS)[:-1])

kernel_name = "hybrid_mla_dsa_peer_block"

def rmsnorm(x, g):
    xf = x.astype(jnp.float32)
    y = xf * lax.rsqrt(jnp.mean(xf * xf, axis=-1, keepdims=True) + EPS)
    return (y * g.astype(jnp.float32)).astype(x.dtype)

def rope(x, pos):
    half = MLA_ROPE // 2
    freqs = ROPE_THETA ** (-2.0 * jnp.arange(half, dtype=jnp.float32) / MLA_ROPE)
    ang = pos.astype(jnp.float32)[:, None] * freqs[None, :]
    cos = jnp.cos(ang)[None, :, None, :]
    sin = jnp.sin(ang)[None, :, None, :]
    xf = x.astype(jnp.float32)
    x1, x2 = xf[..., :half], xf[..., half:]
    return jnp.concatenate([x1 * cos - x2 * sin, x1 * sin + x2 * cos], axis=-1).astype(x.dtype)

def to_blocks(a):
    b, s = a.shape[:2]
    return jnp.moveaxis(a.reshape((b, s // QBLOCK, QBLOCK) + a.shape[2:]), 1, 0)

def from_blocks(a):
    n, b, t = a.shape[:3]
    return jnp.moveaxis(a, 0, 1).reshape((b, n * t) + a.shape[3:])

def t5_bucket(rel):
    nb = REL_BUCKETS // 2
    max_exact = nb // 2
    ret = jnp.where(rel > 0, nb, 0)
    n = jnp.abs(rel)
    nf = jnp.maximum(n, 1).astype(jnp.float32)
    large = max_exact + (jnp.log(nf / max_exact) / math.log(REL_MAX_DIST / max_exact)
                         * (nb - max_exact)).astype(jnp.int32)
    large = jnp.minimum(large, nb - 1)
    return ret + jnp.where(n < max_exact, n, large)

def mla_attention(c_q, c_kv, k_rope, g_cq, g_ckv, w_uq, w_ukv, g_qn, g_kn, pos):
    b, s, _ = c_q.shape
    q = (rmsnorm(c_q, g_cq) @ w_uq).reshape(b, s, MLA_HEADS, MLA_QK)
    kv = (rmsnorm(c_kv, g_ckv) @ w_ukv).reshape(b, s, MLA_HEADS, MLA_NOPE + MLA_V)
    k_nope, v = kv[..., :MLA_NOPE], kv[..., MLA_NOPE:]
    k = jnp.concatenate([k_nope, jnp.broadcast_to(k_rope[:, :, None, :], (b, s, MLA_HEADS, MLA_ROPE))], axis=-1)
    q = rmsnorm(q, g_qn)
    k = rmsnorm(k, g_kn)
    q = jnp.concatenate([q[..., :MLA_NOPE], rope(q[..., MLA_NOPE:], pos)], axis=-1)
    k = jnp.concatenate([k[..., :MLA_NOPE], rope(k[..., MLA_NOPE:], pos)], axis=-1)
    key_chunk = pos // CHUNK
    scale = MLA_QK ** -0.5

    def block(args):
        qb, tb = args
        sc = jnp.einsum('bthd,bshd->bhts', qb, k, preferred_element_type=jnp.float32) * scale
        mask = key_chunk[None, :] <= (tb // CHUNK)[:, None]
        sc = jnp.where(mask[None, None], sc, -jnp.inf)
        p = jax.nn.softmax(sc, axis=-1)
        return jnp.einsum('bhts,bshd->bthd', p.astype(v.dtype), v)

    out = lax.map(block, (to_blocks(q), pos.reshape(-1, QBLOCK)))
    return from_blocks(out).reshape(b, s, MLA_HEADS * MLA_V)

def dsa_attention(q, k, v, q_idx, k_idx, w_idx, g_qn, g_kn, rel_bias, pos):
    b, s, _ = q.shape
    q = rmsnorm(q.reshape(b, s, DSA_HEADS, DSA_HD), g_qn)
    k = rmsnorm(k.reshape(b, s, DSA_HEADS, DSA_HD), g_kn)
    v = v.reshape(b, s, DSA_HEADS, DSA_HD)
    q_idx = q_idx.reshape(b, s, IDX_HEADS, IDX_HD)
    n_sel = min(DSA_TOPK, s // 4)
    key_chunk = pos // CHUNK
    scale = DSA_HD ** -0.5
    idx_scale = IDX_HD ** -0.5
    gather = jax.vmap(lambda a, i: a[i])

    def block(args):
        qb, qib, wb, tb = args
        dots = jnp.einsum('bthd,bsd->bths', qib, k_idx, preferred_element_type=jnp.float32) * idx_scale
        index_score = jnp.einsum('bth,bths->bts', wb.astype(jnp.float32), jax.nn.relu(dots))
        admissible = key_chunk[None, :] <= (tb // CHUNK)[:, None]
        index_score = jnp.where(admissible[None], index_score, -jnp.inf)
        _, sel = lax.top_k(index_score, n_sel)
        valid = (sel // CHUNK) <= (tb // CHUNK)[None, :, None]
        ks = gather(k, sel)
        vs = gather(v, sel)
        bias = rel_bias[t5_bucket(sel - tb[None, :, None])]
        logits = (jnp.einsum('bthd,btkhd->bhtk', qb, ks, preferred_element_type=jnp.float32) * scale
                  + jnp.moveaxis(bias, -1, 1).astype(jnp.float32))
        logits = jnp.where(valid[:, None], logits, -jnp.inf)
        p = jax.nn.softmax(logits, axis=-1)
        return jnp.einsum('bhtk,btkhd->bthd', p.astype(vs.dtype), vs)

    out = lax.map(block, (to_blocks(q), to_blocks(q_idx), to_blocks(w_idx), pos.reshape(-1, QBLOCK)))
    return from_blocks(out).reshape(b, s, DSA_HEADS * DSA_HD)

def peer(h, w_pq, sub_keys, u_tab, v_tab):
    def block(hb):
        b, t, _ = hb.shape
        qr = (hb @ w_pq).reshape(b, t, PEER_HEADS, 2, PEER_DKEY // 2)
        sc = jnp.einsum('bthpd,hpnd->bthpn', qr, sub_keys, preferred_element_type=jnp.float32)
        s_top, i_top = lax.top_k(sc, PEER_TOPK)
        cand = s_top[..., 0, :, None] + s_top[..., 1, None, :]
        c_top, c_pos = lax.top_k(cand.reshape(b, t, PEER_HEADS, PEER_TOPK * PEER_TOPK), PEER_TOPK)
        i0 = jnp.take_along_axis(i_top[..., 0, :], c_pos // PEER_TOPK, axis=-1)
        i1 = jnp.take_along_axis(i_top[..., 1, :], c_pos % PEER_TOPK, axis=-1)
        expert = i0 * PEER_NKEYS + i1
        g = jax.nn.softmax(c_top, axis=-1)
        u = u_tab[expert]
        a = jax.nn.gelu(jnp.einsum('bthkd,btd->bthk', u, hb, preferred_element_type=jnp.float32),
                        approximate=False)
        return jnp.einsum('bthk,bthkd->btd', (g * a).astype(v_tab.dtype), v_tab[expert])

    return from_blocks(lax.map(block, to_blocks(h)))

def setup_inputs(seed: int = 0) -> dict:
    key = jax.random.key(seed)
    ks = jax.random.split(key, 20)
    f32 = jnp.float32

    def nrm(k, shape, scale):
        return jax.random.normal(k, shape, f32) * scale

    def gain(k, shape):
        return 1.0 + 0.01 * jax.random.normal(k, shape, f32)

    return {
        "x": nrm(ks[0], (BATCH, SEQ, D_MODEL), 1.0),
        "g_attn": gain(ks[1], (DEPTH, D_MODEL)),
        "w_in": nrm(ks[2], (DEPTH, D_MODEL, IN_WIDTH), D_MODEL ** -0.5),
        "g_cq": gain(ks[3], (DEPTH, Q_LORA)),
        "g_ckv": gain(ks[4], (DEPTH, KV_LORA)),
        "w_uq": nrm(ks[5], (DEPTH, Q_LORA, MLA_HEADS * MLA_QK), Q_LORA ** -0.5),
        "w_ukv": nrm(ks[6], (DEPTH, KV_LORA, MLA_HEADS * (MLA_NOPE + MLA_V)), KV_LORA ** -0.5),
        "g_mla_q": gain(ks[7], (DEPTH, MLA_QK)),
        "g_mla_k": gain(ks[8], (DEPTH, MLA_QK)),
        "g_dsa_q": gain(ks[9], (DEPTH, DSA_HD)),
        "g_dsa_k": gain(ks[10], (DEPTH, DSA_HD)),
        "rel_bias": nrm(ks[11], (REL_BUCKETS, DSA_HEADS), 0.5),
        "w_o": nrm(ks[12], (DEPTH, MIX_WIDTH, D_MODEL), MIX_WIDTH ** -0.5),
        "g_ffn": gain(ks[13], (DEPTH, D_MODEL)),
        "w_pq": nrm(ks[14], (DEPTH, D_MODEL, PEER_HEADS * PEER_DKEY), D_MODEL ** -0.5),
        "sub_keys": nrm(ks[15], (DEPTH, PEER_HEADS, 2, PEER_NKEYS, PEER_DKEY // 2), (PEER_DKEY // 2) ** -0.5),
        "u_tab": nrm(ks[16], (DEPTH, PEER_EXPERTS, D_MODEL), D_MODEL ** -0.5),
        "v_tab": nrm(ks[17], (DEPTH, PEER_EXPERTS, D_MODEL), PEER_HEADS ** -0.5),
    }

def reference(x, g_attn, w_in, g_cq, g_ckv, w_uq, w_ukv, g_mla_q, g_mla_k, g_dsa_q, g_dsa_k,
              rel_bias, w_o, g_ffn, w_pq, sub_keys, u_tab, v_tab):
    s = x.shape[1]
    pos = jnp.arange(s, dtype=jnp.int32)
    for l in range(DEPTH):
        h = rmsnorm(x, g_attn[l])
        proj = h @ w_in[l]
        c_q, c_kv, k_rope, q_d, k_d, v_d, q_i, k_i, w_i = jnp.split(proj, IN_OFFSETS, axis=-1)
        y_a = mla_attention(c_q, c_kv, k_rope, g_cq[l], g_ckv[l], w_uq[l], w_ukv[l],
                            g_mla_q[l], g_mla_k[l], pos)
        y_b = dsa_attention(q_d, k_d, v_d, q_i, k_i, w_i, g_dsa_q[l], g_dsa_k[l], rel_bias, pos)
        x = x + jnp.concatenate([y_a, y_b], axis=-1) @ w_o[l]
        x = x + peer(rmsnorm(x, g_ffn[l]), w_pq[l], sub_keys[l], u_tab[l], v_tab[l])
    return x


_drawn_inputs = setup_inputs


def setup_inputs(seed=0):
    import zlib

    import numpy as np

    out = dict(_drawn_inputs(seed))
    spreads = {}
    factors = {'g_cq': 8.0,
     'g_ckv': 7.848,
     'g_mla_q': 8.0,
     'g_mla_k': 8.0,
     'g_dsa_q': 41.918,
     'g_dsa_k': 42.111,
     'g_ffn': 24.16,
     'rel_bias': 6.302}
    for name, (base, spread) in spreads.items():
        noise = np.random.default_rng([zlib.crc32(name.encode()), seed]).standard_normal(out[name].shape)
        drawn = base * np.exp(spread * noise) if base else spread * noise
        out[name] = __import__('jax').numpy.asarray(drawn.astype(out[name].dtype))
    for name, factor in factors.items():
        out[name] = (out[name] * factor).astype(out[name].dtype)
    return out
```

```python
import math
from contextlib import ExitStack

import concourse.bass as bass
import numpy as np
from concourse import mybir


def build_block(nc, io):
    F32 = mybir.dt.float32
    F32R = mybir.dt.float32r
    U32 = mybir.dt.uint32
    ALU = mybir.AluOpType
    ACT = mybir.ActivationFunctionType
    AX = mybir.AxisListType.X
    ds = bass.ds

    P = 128
    SEQ, D = io["x"].shape
    TT = SEQ // P
    KD = D // P
    IN_W = io["w_in"].shape[1]
    QL, CKV, ROPE = 512, 256, 64
    NH, NOPE, HD = 8, 128, 128
    QK = NOPE + ROPE
    IH, ID = 16, 64
    N_SEL = SEQ // 4
    TOPK, NKEY = 16, 128
    EPS = 1e-6
    MASKED, REMOVED = -1.0e30, -3.0e38
    O_CQ, O_CKV, O_KR = 0, QL, QL + CKV
    O_QD = O_KR + ROPE
    O_KD = O_QD + NH * HD
    O_VD = O_KD + NH * HD
    O_QI = O_VD + NH * HD
    O_KI = O_QI + IH * ID
    O_WI = O_KI + ID
    assert O_WI + IH == IN_W

    UNIT = 1024
    NRAW, NPART = 4, 2
    N_IN = -(-IN_W // 512)
    LAST_W = IN_W - 512 * (N_IN - 1)
    U_IN, U_WO, U_PQ = 8 * N_IN, 8 * (D // 512), 2 * 16
    B_IN = 0
    B_WO = B_IN + U_IN
    B_PQ = B_WO + U_WO
    B_U = B_PQ + U_PQ
    B_V = B_U + 2 * NKEY
    B_END = B_V + 2 * NKEY

    with ExitStack() as ctx:
        def sb(name, shape, dt=F32):
            return ctx.enter_context(nc.sbuf_tensor(name, shape, dt))

        def sem(name):
            return ctx.enter_context(nc.semaphore(name))

        acts = sb("acts", [P, NKEY * SEQ])
        hT_hi = sb("hT_hi", [P, KD, SEQ], F32R)
        hT_lo = sb("hT_lo", [P, KD, SEQ], F32R)
        raw = [sb(f"raw{i}", [P, UNIT]) for i in range(NRAW)]
        whi = [sb(f"w_hi{i}", [P, UNIT], F32R) for i in range(NPART)]
        wlo = [sb(f"w_lo{i}", [P, UNIT], F32R) for i in range(NPART)]
        ehi = [sb(f"e_hi{i}", [P, SEQ], F32R) for i in range(2)]
        elo = [sb(f"e_lo{i}", [P, SEQ], F32R) for i in range(2)]
        ident = sb("ident", [P, P])
        iota = sb("iota", [P, P])
        eps = sb("eps", [P, 1])
        gains = sb("gains", [P, 2 * KD + 10])
        slotT = sb("slotT", [P, 3, SEQ])
        early = sb("early", [P, 1536])
        stat = sb("stat", [P, 288])
        ps = ctx.enter_context(nc.psum_tensor("ps", [P, 8, 512], F32))

        G_ATTN, G_FFN, G_CQ, G_CKV, G_MQ, G_MK, G_DQ, G_DK = 0, KD, 2 * KD, 2 * KD + 4, 2 * KD + 6, 2 * KD + 7, 2 * KD + 8, 2 * KD + 9

        ckvT = early[:, 0:512].rearrange("p (k t) -> p k t", k=2)
        chunk_mask = early[:, 512:1024].rearrange("p (b s) -> p b s", b=TT)
        kpad = early[:, 1024:1280].rearrange("p (r d) -> p r d", r=2)
        rope_tab = early[:, 1280:1408].rearrange("p (f b c) -> p f b c", f=2, b=TT)
        rope_gain = early[:, 1408:1536].rearrange("p (f c) -> p f c", f=2)
        krot = early[:, 0:512]
        hot1 = [early[:, 128 * i:128 * i + 128] for i in range(4)]
        hot0 = [early[:, 512 + 128 * i:512 + 128 * i + 128] for i in range(4)]

        def region(at, n):
            return acts[:, at:at + n]

        proj = [region(b * IN_W, IN_W) for b in range(TT)]
        A_WU = TT * IN_W
        w_uq = region(A_WU, 6144).rearrange("p (k n) -> p k n", k=4)
        w_ukv = region(A_WU + 6144, 4096).rearrange("p (k n) -> p k n", k=2)
        head_view = lambda at, n=8: region(at, n * SEQ).rearrange("p (h t) -> p h t", h=n)
        qTn, qTr, kTn = head_view(A_WU), head_view(A_WU + 2048), head_view(A_WU + 4096)
        kTr = head_view(A_WU + 6144, 4)
        qiT = head_view(A_WU + 7168)
        kiT = head_view(A_WU + 9216, 2)
        A_KV = A_WU + 10240
        kv = [region(A_KV + 2048 * b, 2048) for b in range(TT)]
        A_BIAS = A_KV + 4096
        bias = [region(A_BIAS + 2048 * b, 2048).rearrange("p (h s) -> p h s", h=NH) for b in range(TT)]
        A_QM = A_BIAS + 4096
        qm = [region(A_QM + 1536 * b, 1536) for b in range(TT)]
        A_TAIL = A_QM + 3072
        cqT = region(A_TAIL, 1024).rearrange("p (k t) -> p k t", k=4)
        qpad = region(A_TAIL, 1024)
        qdT, kdT = head_view(A_QM), head_view(A_QM + 2048)
        assert A_TAIL + 1024 <= NKEY * SEQ
        rope_tmp = [proj[0][:, 256 * i:256 * i + 256] for i in range(3)] + [proj[1][:, 0:256], proj[1][:, 256:320]]
        relu_buf = [proj[0][:, O_QD + 512 * i:O_QD + 512 * i + 512] for i in range(2)]
        work = [proj[1][:, O_QD + 256 * b:O_QD + 256 * b + 256] for b in range(TT)]
        logit = [proj[0][:, O_KD + 512 * i:O_KD + 512 * i + 512] for i in range(2)]
        probT = [proj[1][:, O_KD + 512 * i:O_KD + 512 * i + 512] for i in range(2)]
        bias_vec = region(A_WU, 512)
        xs = [region(D * b, D) for b in range(TT)]
        xn = [region(TT * D + D * b, D) for b in range(TT)]
        qr = region(2 * TT * D, 16 * SEQ).rearrange("p (c t) -> p c t", c=16)
        subk = region(2 * TT * D + 16 * SEQ, 16 * NKEY).rearrange("p (c n) -> p c n", c=16)
        A_TK = 20480
        cand = region(A_TK, 2048)
        pick = region(A_TK + 2048, 2048)
        top_v = region(A_TK + 4096, 256).rearrange("p (c j) -> p c j", c=16)
        top_iu = region(A_TK + 4352, 256).bitcast(U32).rearrange("p (c j) -> p c j", c=16)
        top_i = region(A_TK + 4608, 256).rearrange("p (c j) -> p c j", c=16)
        c_v = region(A_TK + 4864, 128).rearrange("p (h j) -> p h j", h=NH)
        c_iu = region(A_TK + 4992, 128).bitcast(U32).rearrange("p (h j) -> p h j", h=NH)
        c_digit_u = region(A_TK + 5120, 256).bitcast(U32).rearrange("p (f h j) -> p f h j", f=2, h=NH)
        c_digit = region(A_TK + 5376, 256).rearrange("p (f h j) -> p f h j", f=2, h=NH)
        slot = region(A_TK + 5632, 384).rearrange("p (f s) -> p f s", f=3)
        gate_sum = region(A_TK + 6016, 16)
        score = [region(A_TK + 8192 + 2048 * b, 2048).rearrange("p (c n) -> p c n", c=16) for b in range(TT)]
        acts_e = acts[:, :].rearrange("p (e t) -> p e t", t=SEQ)

        ss_x, rs_x = stat[:, 0:2], stat[:, 2:4]
        ss_c, rs_c = stat[:, 4:8], stat[:, 8:12]
        ss_kr = stat[:, 12:14]
        ss_h = stat[:, 16:80].rearrange("p (b k h) -> p b k h", b=TT, k=4)
        rs_h = stat[:, 80:144].rearrange("p (b k h) -> p b k h", b=TT, k=4)
        j_max, j_nmax = stat[:, 144:176], stat[:, 176:208]
        j_sum, j_rec = stat[:, 208:240], stat[:, 240:272]
        top8 = stat[:, 272:280]

        raw_ready = [sem(f"raw_ready{i}") for i in range(NRAW)]
        hi_done, lo_done, unit_used = sem("hi_done"), sem("lo_done"), sem("unit_used")
        x_in, const_in, gain_in, mask_in, wu_in = sem("x_in"), sem("const_in"), sem("gain_in"), sem("mask_in"), sem("wu_in")
        hot_in, vec_mm, vec_ready, vec_out, bias_in = sem("hot_in"), sem("vec_mm"), sem("vec_ready"), sem("vec_out"), sem("bias_in")
        x_back, subk_in, x2_done, x2_stored, x2_back = sem("x_back"), sem("subk_in"), sem("x2_done"), sem("x2_stored"), sem("x2_back")
        x_root, xn_done, xT_mm, hThi_done, hTlo_done = sem("x_root"), sem("xn_done"), sem("xT_mm"), sem("hThi_done"), sem("hTlo_done")
        proj_done = sem("proj_done")
        c_root, cn_done, cT_mm, cT_done, up_mm, up_done = sem("c_root"), sem("cn_done"), sem("cT_mm"), sem("cT_done"), sem("up_mm"), sem("up_done")
        sq_done, red_done, ss_done, h_root = sem("sq_done"), sem("red_done"), sem("ss_done"), sem("h_root")
        tok_ready, headT_mm, headT_done = sem("tok_ready"), sem("headT_mm"), sem("headT_done")
        dot_mm, relu_done, acc_done = sem("dot_mm"), sem("relu_done"), sem("acc_done")
        logit_mm, logit_done, exp_done, prob_done = sem("logit_mm"), sem("logit_done"), sem("exp_done"), sem("prob_done")
        pT_mm, pT_done, y_mm, yhi_done, ylo_done = sem("pT_mm"), sem("pT_done"), sem("y_mm"), sem("yhi_done"), sem("ylo_done")
        qr_done, score_mm, score_done = sem("qr_done"), sem("score_mm"), sem("score_done")
        cmax_done, cexp_done, slot_done, slotT_mm, slotT_done = sem("cmax_done"), sem("cexp_done"), sem("slot_done"), sem("slotT_mm"), sem("slotT_done")
        gelu_done, hot_done, gate_mm, gated = sem("gelu_done"), sem("hot_done"), sem("gate_mm"), sem("gated")
        ehi_done, elo_done, out_ready, out_sent = sem("ehi_done"), sem("elo_done"), sem("out_ready"), sem("out_sent")
        dve_chain, act_chain = sem("dve_chain"), sem("act_chain")

        JOBS = [(g, pr, b) for g in range(2) for pr in range(NH // 2) for b in range(TT)]
        kv_h = [kv[b].rearrange("p (h d) -> p h d", h=NH) for b in range(TT)]
        qm_h = [qm[b].rearrange("p (h d) -> p h d", h=NH) for b in range(TT)]

        def tile_groups():
            for b in range(TT):
                t = slice(b * P, b * P + P)
                for g in range(2):
                    yield [qm_h[b][:, 4 * g + i, 0:NOPE] for i in range(4)], qTn[:, 4 * g:4 * g + 4, t], G_MQ, 2 * b + 1
                for g in range(2):
                    yield [proj[b][:, O_QI + 128 * (4 * g + i):O_QI + 128 * (4 * g + i) + 128] for i in range(4)], qiT[:, 4 * g:4 * g + 4, t], None, 2 * b + 1
                yield [kpad[:, r, :] for r in range(2)], kiT[:, :, t], None, 2 * b + 1
                for g in range(2):
                    yield [kv_h[b][:, 4 * g + i, 0:NOPE] for i in range(4)], kTn[:, 4 * g:4 * g + 4, t], G_MK, 2 * b + 2
                yield [krot[:, 128 * i:128 * i + 128] for i in range(4)], kTr[:, :, t], None, 2 * b + 2
                for g in range(2):
                    yield [qpad[:, 128 * (4 * g + i):128 * (4 * g + i) + 128] for i in range(4)], qTr[:, 4 * g:4 * g + 4, t], None, 2 * b + 2
            for b in range(TT):
                t = slice(b * P, b * P + P)
                for off, dst, gain in ((O_QD, qdT, G_DQ), (O_KD, kdT, G_DK)):
                    for g in range(2):
                        yield [proj[b][:, off + 128 * (4 * g + i):off + 128 * (4 * g + i) + 128] for i in range(4)], dst[:, 4 * g:4 * g + 4, t], gain, 2 * TT
        GROUPS = list(tile_groups())
        GROUPS_OF_TILE = 10

        SQUARES = []
        for b, banks in enumerate(((0, 3, 5, 0), (2, 5, 0, 2))):
            SQUARES += [(qm_h[b], banks[0], 3, b, 0), (kv_h[b][:, :, 0:NOPE], banks[1], 2, b, 1),
                        (proj[b][:, O_QD:O_KD].rearrange("p (h d) -> p h d", h=NH), banks[2], 2, b, 2),
                        (proj[b][:, O_KD:O_VD].rearrange("p (h d) -> p h d", h=NH), banks[3], 2, b, 3)]

        block = ctx.enter_context(nc.Block())

        def width(n):
            return 512 if not isinstance(n, int) or n < N_IN - 1 else LAST_W

        @block.sync
        def _(sp):
            def load(u, j, src):
                if not (isinstance(u, int) and u < NRAW):
                    sp.wait_ge(lo_done, u - (NRAW - 1))
                dst = raw[j % NRAW][:, 0:src.free_size()]
                if len(src.shape) == 3:
                    dst = dst.rearrange("p (k n) -> p k n", k=src.shape[1])
                sp.dma_start(dst, src).then_inc(raw_ready[j % NRAW], 16)

            sp.dma_start(acts[:, 0:TT * D].rearrange("p (b d) -> p b d", b=TT), io["x"].rearrange("(b p) d -> p b d", p=P)).then_inc(x_in, 16)
            sp.dma_start(ident[:, :], io["ident"]).then_inc(const_in, 16)
            sp.dma_start(eps[:, :], io["eps"]).then_inc(gain_in, 16)
            sp.dma_start(gains[:, :], io["gains"]).then_inc(gain_in, 16)
            win = io["w_in"].rearrange("(k p) n -> p k n", p=P)
            for j in range(8):
                load(j, j, win[:, 2 * j:2 * j + 2, 0:512])
            with sp.Fori(1, N_IN - 1) as n:
                for j in range(8):
                    load(n * 8 + j, j, win[:, 2 * j:2 * j + 2, ds(n * 512, 512)])
            for j in range(8):
                load(B_IN + 8 * (N_IN - 1) + j, j, win[:, 2 * j:2 * j + 2, 512 * (N_IN - 1):IN_W])
            wo = io["w_o"].rearrange("(k p) n -> p k n", p=P)
            with sp.Fori(0, D // 512) as n:
                for j in range(8):
                    load(n * 8 + (B_WO + j), j, wo[:, 2 * j:2 * j + 2, ds(n * 512, 512)])
            with sp.Fori(0, U_PQ // 4) as i:
                for j in range(4):
                    load(i * 4 + (B_PQ + j), j, io["w_pq"][ds(i * (4 * P) + j * P, P), :])
            with sp.Fori(0, 2 * NKEY // 4) as i:
                for j in range(4):
                    load(i * 4 + (B_U + j), j, io["u_tab"][ds(i * (4 * P) + j * P, P), :])
            with sp.Fori(0, 2 * NKEY // 4) as i:
                for j in range(4):
                    load(i * 4 + (B_V + j), j,
                         io["v_tab"][ds(i * (2 * P) + (j // 2) * P, P), (j % 2) * UNIT:(j % 2) * UNIT + UNIT])
            for g in range(8):
                b, n = g // 4, g % 4
                sp.wait_ge(out_ready, g + 1)
                sp.dma_start(io["out"][b * P:b * P + P, n * 512:n * 512 + 512], xn[b][:, n * 512:n * 512 + 512]).then_inc(out_sent, 16)
            sp.wait_ge(out_sent, 16 * 8)
            sp.wait_ge(x2_stored, 16)
            sp.wait_ge(vec_out, 16)

        @block.gpsimd
        def _(pool):
            pool.dma_start(acts[0:32, A_BIAS:A_BIAS + 512], io["bucket_hot"]).then_inc(hot_in, 16)
            pool.dma_start(acts[0:32, A_BIAS + 512:A_BIAS + 520], io["rel_bias"]).then_inc(hot_in, 16)
            pool.dma_start(iota[:, :], io["iota"]).then_inc(mask_in, 16)
            pool.dma_start(early[:, 1280:1408], io["rope_tab"]).then_inc(mask_in, 16)
            pool.dma_start(early[:, 512:1024], io["chunk_mask"]).then_inc(mask_in, 16)
            pool.dma_start(early[:, 1408:1536], io["rope_gain"].to_broadcast([P, 128])).then_inc(mask_in, 16)
            pool.wait_ge(vec_ready, 1)
            pool.dma_start(io["bias_scratch"], acts[0:8, A_WU:A_WU + 512].unsqueeze(1).to_broadcast([8, P, 512])).then_inc(vec_out, 16)
            pool.wait_ge(vec_out, 16)
            for b in range(TT):
                first = SEQ - 1 - b * P
                src = bass.AP(io["bias_scratch"].tensor, first, [[511, P], [512 * P, NH], [1, SEQ]])
                pool.dma_start(bias[b], src).then_inc(bias_in, 16)
            pool.dma_start(w_uq, io["w_uq"].rearrange("(k p) n -> p k n", p=P)).then_inc(wu_in, 16)
            pool.dma_start(w_ukv, io["w_ukv"].rearrange("(k p) n -> p k n", p=P)).then_inc(wu_in, 16)
            pool.wait_ge(ylo_done, len(JOBS))
            pool.dma_start(acts[:, 0:TT * D].rearrange("p (b d) -> p b d", b=TT), io["x"].rearrange("(b p) d -> p b d", p=P)).then_inc(x_back, 16)
            pool.dma_start(subk, io["sub_keys"]).then_inc(subk_in, 16)
            pool.wait_ge(x2_done, 8)
            pool.dma_start(io["x2_scratch"].rearrange("(b p) d -> p b d", p=P), acts[:, 0:TT * D].rearrange("p (b d) -> p b d", b=TT)).then_inc(x2_stored, 16)
            pool.wait_ge(x2_stored, 16)
            pool.wait_ge(unit_used, B_V + 4 * TT * D // SEQ)
            pool.dma_start(acts[:, 0:TT * D].rearrange("p (b d) -> p b d", b=TT), io["x2_scratch"].rearrange("(b p) d -> p b d", p=P)).then_inc(x2_back, 16)

        @block.scalar
        def _(act):
            links = [0]

            def link(*ins):
                for i in ins:
                    i.then_inc(act_chain, 1)
                links[0] += len(ins)
                act.wait_ge(act_chain, links[0])

            def split_hi(u, j, w=UNIT):
                fill = u // NRAW if isinstance(u, int) else None
                act.wait_ge(raw_ready[j % NRAW], (u - j % NRAW) * (16 // NRAW) + 16)
                if not (isinstance(u, int) and u < NPART):
                    act.wait_ge(unit_used, u - (NPART - 1))
                nc.scalar.activation(whi[j % NPART][:, 0:w], raw[j % NRAW][:, 0:w], ACT.Copy).then_inc(hi_done, 1)

            def norm_root():
                link(*[nc.scalar.activation(xn[b], xs[b], ACT.Square, accum_out=ss_x[:, b:b + 1]) for b in range(TT)])
                nc.scalar.activation(rs_x, ss_x, ACT.Sqrt, bias=eps[:, :], scale=1.0 / D).then_inc(x_root, 1)

            def norm_hi(first, gain):
                for k in range(KD):
                    act.wait_ge(xT_mm, first + k + 1)
                    nc.scalar.activation(hT_hi[:, k, :], ps[:, k % 8, 0:SEQ], ACT.Copy,
                                         scale=gains[:, gain + k:gain + k + 1]).then_inc(hThi_done, 1)

            act.wait_ge(x_in, 16)
            act.wait_ge(gain_in, 32)
            norm_root()
            norm_hi(0, G_ATTN)

            def proj_out(n, par):
                act.wait_ge(unit_used, n * 8 + 8)
                for b in range(TT):
                    ins = nc.scalar.activation(acts[:, ds(n * 512 + b * IN_W, width(n))], ps[:, 2 * par + b, 0:width(n)], ACT.Copy)
                ins.then_inc(proj_done, 1)

            def in_block(n, par):
                for j in range(8):
                    split_hi(n * 8 + j, j, 2 * width(n))
                    if j == 1 and not (isinstance(n, int) and n == 0):
                        proj_out(n - 1, 1 - par)
            in_block(0, 0)
            in_block(1, 1)
            with act.Fori(1, N_IN // 2 - 1) as i:
                in_block(i * 2, 0)
                in_block(i * 2 + 1, 1)
            in_block(N_IN - 2, 0)
            in_block(N_IN - 1, 1)
            proj_out(N_IN - 1, 1)
            act.wait_ge(proj_done, N_IN)

            squares = []
            for b in range(TT):
                squares.append(nc.scalar.activation(ps[:, 4 + 2 * b, :], proj[b][:, O_CQ:O_CQ + QL], ACT.Square, accum_out=ss_c[:, b:b + 1]))
                squares.append(nc.scalar.activation(ps[:, 5 + 2 * b, 0:CKV], proj[b][:, O_CKV:O_CKV + CKV], ACT.Square, accum_out=ss_c[:, 2 + b:3 + b]))
            link(*squares)
            nc.scalar.activation(rs_c[:, 0:2], ss_c[:, 0:2], ACT.Sqrt, bias=eps[:, :], scale=1.0 / QL).then_inc(c_root, 1)
            nc.scalar.activation(rs_c[:, 2:4], ss_c[:, 2:4], ACT.Sqrt, bias=eps[:, :], scale=1.0 / CKV).then_inc(c_root, 1)
            for k in range(6):
                act.wait_ge(cT_mm, k + 1)
                dst, gain = (cqT[:, k, :], G_CQ + k) if k < 4 else (ckvT[:, k - 4, :], G_CKV + k - 4)
                nc.scalar.activation(dst, ps[:, k, 0:SEQ], ACT.Copy,
                                     scale=gains[:, gain:gain + 1]).then_inc(cT_done, 1)
            for g in range(14):
                b, n = g // 7, g % 7
                act.wait_ge(up_mm, g + 1)
                dst = qm[b][:, n * 512:n * 512 + 512] if n < 3 else kv[b][:, (n - 3) * 512:(n - 3) * 512 + 512]
                nc.scalar.activation(dst, ps[:, g % 8, :], ACT.Copy).then_inc(up_done, 1)
            act.wait_ge(up_done, 14)

            link(*[nc.scalar.activation(ps[:, 7, b * ROPE:b * ROPE + ROPE], proj[b][:, O_KR:O_KR + ROPE], ACT.Square, accum_out=ss_kr[:, b:b + 1]) for b in range(TT)])
            for i, (src, bank, banks, b, kind) in enumerate(SQUARES):
                if i >= 3:
                    act.wait_ge(red_done, i - 2)
                n = src.free_size()
                dst = ps[:, bank:bank + banks, :].rearrange("p a n -> p (a n)")[:, 0:n].rearrange("p (h d) -> p h d", h=NH)
                nc.scalar.activation(dst, src, ACT.Square).then_inc(sq_done, 1)
            act.wait_ge(ss_done, 2)
            for kind, n in ((0, QK), (1, QK), (2, HD), (3, HD)):
                nc.scalar.activation(rs_h[:, :, kind, :], ss_h[:, :, kind, :], ACT.Sqrt, bias=eps[:, :], scale=1.0 / n).then_inc(h_root, 1)

            for g, (srcs, dst, gain, _) in enumerate(GROUPS):
                act.wait_ge(headT_mm, g + 1)
                src = ps[:, g % 8, 0:128 * len(srcs)].rearrange("p (h t) -> p h t", t=P)
                scale = 1.0 if gain is None else gains[:, gain:gain + 1]
                nc.scalar.activation(dst, src, ACT.Copy, scale=scale).then_inc(headT_done, 1)

            for c in range(TT * IH // 2):
                S = P * (c // (IH // 2) + 1)
                act.wait_ge(dot_mm, c + 1)
                if c >= 2:
                    act.wait_ge(acc_done, c - 1)
                nc.scalar.activation(relu_buf[c % 2][:, 0:2 * S], ps[:, 6 + c % 2, 0:2 * S], ACT.Relu, scale=ID ** -0.5).then_inc(relu_done, 1)

            def exps(j):
                S = P * (JOBS[j][2] + 1)
                act.wait_ge(logit_done, j + 1)
                for hh in range(2):
                    part = logit[j % 2][:, hh * S:hh * S + S]
                    ins = nc.scalar.activation(part, part, ACT.Exp, bias=j_nmax[:, 2 * j + hh:2 * j + hh + 1],
                                               accum_out=j_sum[:, 2 * j + hh:2 * j + hh + 1])
                ins.then_inc(exp_done, 1)

            def probT_out(j):
                S = P * (JOBS[j][2] + 1)
                act.wait_ge(pT_mm, j + 1)
                if j >= 2:
                    act.wait_ge(y_mm, j - 1)
                nc.scalar.activation(probT[j % 2][:, 0:2 * S], ps[:, 2 + j % 2, 0:2 * S], ACT.Copy).then_inc(pT_done, 1)

            def y_hi(j):
                g, pr, b = JOBS[j]
                k = g * NH + 2 * pr
                act.wait_ge(y_mm, j + 1)
                nc.scalar.activation(hT_hi[:, k:k + 2, b * P:b * P + P], ps[:, 4 + j % 2, 0:256].rearrange("p (h t) -> p h t", h=2),
                                     ACT.Copy).then_inc(yhi_done, 1)
            for step in range(len(JOBS) + 2):
                if step < len(JOBS):
                    exps(step)
                if 1 <= step <= len(JOBS):
                    probT_out(step - 1)
                if step >= 2:
                    y_hi(step - 2)

            with act.Fori(0, U_WO // 4) as i:
                for j in range(4):
                    split_hi(i * 4 + (B_WO + j), j)

            act.wait_ge(x2_done, 8)
            norm_root()
            norm_hi(KD, G_FFN)

            def chunk_pair(i, base, out):
                for j in range(4):
                    split_hi(i * 4 + (base + j), j)
                    if j == 1 and not (isinstance(i, int) and i == 0):
                        out(i * 2 - 1, 1)
                    if j == 3:
                        out(i * 2, 0)

            def queries_out(c, par):
                act.wait_ge(unit_used, c * 2 + (B_PQ + 2))
                nc.scalar.activation(acts[:, ds(c * SEQ + 2 * TT * D, SEQ)], ps[:, par, 0:SEQ], ACT.Copy).then_inc(qr_done, 1)

            chunk_pair(0, B_PQ, queries_out)
            with act.Fori(1, U_PQ // 4) as i:
                chunk_pair(i, B_PQ, queries_out)
            queries_out(15, 1)
            for g in range(8):
                b, q = g // 4, g % 4
                act.wait_ge(score_mm, g + 1)
                nc.scalar.activation(score[b][:, 4 * q:4 * q + 4, :], ps[:, 2 + g % 4, :].rearrange("p (c n) -> p c n", c=4), ACT.Copy).then_inc(score_done, 1)
            for b in range(TT):
                act.wait_ge(cmax_done, b + 1)
                nc.scalar.activation(slot[:, 2, :], slot[:, 2, :], ACT.Exp).then_inc(cexp_done, 1)

            act.wait_ge(x2_stored, 16)
            act.wait_ge(slotT_mm, TT)

            def gelu(c, par):
                act.wait_ge(unit_used, c * 2 + (B_U + 2))
                nc.scalar.activation(acts[:, ds(c * SEQ, SEQ)], ps[:, par, 0:SEQ], ACT.Gelu).then_inc(gelu_done, 1)
            chunk_pair(0, B_U, gelu)
            with act.Fori(1, NKEY // 2) as i:
                chunk_pair(i, B_U, gelu)
            gelu(NKEY - 1, 1)

            act.wait_ge(gated, SEQ // 4)

            def expert_pair(i):
                for j in range(4):
                    if j % 2 == 0:
                        if not (isinstance(i, int) and i == 0):
                            act.wait_ge(unit_used, i * 4 + (B_V + j - 2))
                        nc.scalar.activation(ehi[j // 2][:, :], acts[:, ds(i * (2 * SEQ) + (j // 2) * SEQ, SEQ)], ACT.Copy).then_inc(ehi_done, 1)
                    split_hi(i * 4 + (B_V + j), j)
            expert_pair(0)
            with act.Fori(1, NKEY // 2) as i:
                expert_pair(i)

        @block.vector
        def _(dve):
            links = [0]
            V = nc.vector

            def link(*ins):
                for i in ins:
                    i.then_inc(dve_chain, 1)
                links[0] += len(ins)
                dve.wait_ge(dve_chain, links[0])

            def split_lo(u, j, w=UNIT):
                dve.wait_ge(hi_done, u + 1)
                V.tensor_tensor(wlo[j % NPART][:, 0:w], raw[j % NRAW][:, 0:w], whi[j % NPART][:, 0:w].bitcast(F32), ALU.subtract).then_inc(lo_done, 1)

            def norm_scale(nth):
                dve.wait_ge(x_root, nth + 1)
                link(V.reciprocal(rs_x, rs_x))
                for b in range(TT):
                    V.tensor_scalar(xn[b], xs[b], rs_x[:, b:b + 1], None, ALU.mult).then_inc(xn_done, 1)

            def norm_lo(nth, gain):
                for k in range(KD):
                    dve.wait_ge(hThi_done, nth * KD + k + 1)
                    V.scalar_tensor_tensor(hT_lo[:, k, :], ps[:, k % 8, 0:SEQ], gains[:, gain + k:gain + k + 1],
                                           hT_hi[:, k, :].bitcast(F32), ALU.mult, ALU.subtract).then_inc(hTlo_done, 1)

            link(V.memset(kpad, 0.0))
            dve.wait_ge(vec_mm, 1)
            V.tensor_copy(acts[0:8, A_WU:A_WU + 512], ps[0:8, 7, :]).then_inc(vec_ready, 1)
            norm_scale(0)
            norm_lo(0, G_ATTN)

            with dve.Fori(0, (N_IN - 1) * 2) as i:
                for j in range(4):
                    split_lo(i * 4 + j, j)
            for j in range(8):
                split_lo(8 * (N_IN - 1) + j, j, 2 * LAST_W)

            dve.wait_ge(c_root, 2)
            link(V.reciprocal(rs_c, rs_c))
            for b in range(TT):
                V.tensor_scalar(proj[b][:, O_CQ:O_CQ + QL], proj[b][:, O_CQ:O_CQ + QL], rs_c[:, b:b + 1], None, ALU.mult).then_inc(cn_done, 1)
                V.tensor_scalar(proj[b][:, O_CKV:O_CKV + CKV], proj[b][:, O_CKV:O_CKV + CKV], rs_c[:, 2 + b:3 + b], None, ALU.mult).then_inc(cn_done, 1)

            for i, (src, bank, banks, b, kind) in enumerate(SQUARES):
                dve.wait_ge(sq_done, i + 1)
                n = src.free_size()
                sq = ps[:, bank:bank + banks, :].rearrange("p a n -> p (a n)")[:, 0:n].rearrange("p (h d) -> p h d", h=NH)
                V.tensor_reduce(ss_h[:, b, kind, :], sq, AX, ALU.add).then_inc(red_done, 1)
            dve.wait_ge(red_done, len(SQUARES))
            for b in range(TT):
                V.tensor_scalar(ss_h[:, b, 1, :], ss_h[:, b, 1, :], ss_kr[:, b:b + 1], None, ALU.add).then_inc(ss_done, 1)
            dve.wait_ge(h_root, 4)
            link(V.reciprocal(rs_h, rs_h))
            link(V.tensor_scalar(rs_h[:, :, 0, :], rs_h[:, :, 0, :], QK ** -0.5, None, ALU.mult),
                 V.tensor_scalar(rs_h[:, :, 2, :], rs_h[:, :, 2, :], HD ** -0.5, None, ALU.mult))

            dve.wait_ge(mask_in, 64)
            link(V.memset(qpad, 0.0))
            for b in range(TT):
                if b:
                    dve.wait_ge(headT_mm, 5)
                key = proj[b][:, O_KI:O_KI + ID]
                V.tensor_copy(kpad[:, 0, 0:ID], key)
                V.tensor_copy(kpad[:, 1, ID:2 * ID], key).then_inc(tok_ready, 1)
                def per_head(kind, n):
                    return rs_h[:, b, kind, :].unsqueeze(2).to_broadcast([P, NH, n])
                kn = kv_h[b][:, :, 0:NOPE]
                V.tensor_tensor(kn, kn, per_head(1, NOPE), ALU.mult)
                kd = proj[b][:, O_KD:O_VD].rearrange("p (h d) -> p h d", h=NH)
                V.tensor_tensor(kd, kd, per_head(3, HD), ALU.mult)
                half = ROPE // 2
                qr_ = qm_h[b][:, :, NOPE:QK]
                kr_ = proj[b][:, O_KR:O_KR + ROPE]
                link(V.tensor_tensor(qr_, qr_, rope_gain[:, 0, :].unsqueeze(1).to_broadcast([P, NH, ROPE]), ALU.mult),
                     V.tensor_tensor(kr_, kr_, rope_gain[:, 1, :], ALU.mult))
                tab = [rope_tab[:, f, b, :] for f in range(2)]
                tmp = [rope_tmp[i].rearrange("p (h c) -> p h c", h=NH) for i in range(4)]
                ops = []
                for i, (part, f) in enumerate(((0, 0), (1, 1), (0, 1), (1, 0))):
                    ops.append(V.tensor_tensor(tmp[i], qr_[:, :, part * half:part * half + half], tab[f].unsqueeze(1).to_broadcast([P, NH, half]), ALU.mult))
                link(*ops)
                if b:
                    dve.wait_ge(headT_mm, GROUPS_OF_TILE)
                qp = qpad.rearrange("p (a r d) -> p a r d", r=2, d=128)
                ops = []
                for r in range(2):
                    t4 = [t.rearrange("p (a r) c -> p a r c", r=2)[:, :, r, :] for t in tmp]
                    ops.append(V.tensor_tensor(qp[:, :, r, r * ROPE:r * ROPE + half], t4[0], t4[1], ALU.subtract))
                    ops.append(V.tensor_tensor(qp[:, :, r, r * ROPE + half:r * ROPE + ROPE], t4[2], t4[3], ALU.add))
                link(*ops)
                kt = rope_tmp[0]
                ops = []
                for i, (part, f) in enumerate(((0, 0), (1, 1), (0, 1), (1, 0))):
                    ops.append(V.tensor_tensor(kt[:, i * half:i * half + half], kr_[:, part * half:part * half + half], tab[f], ALU.mult))
                link(*ops)
                rot = rope_tmp[4]
                link(V.tensor_tensor(rot[:, 0:half], kt[:, 0:half], kt[:, half:2 * half], ALU.subtract),
                     V.tensor_tensor(rot[:, half:ROPE], kt[:, 2 * half:3 * half], kt[:, 3 * half:4 * half], ALU.add))
                V.tensor_tensor(krot.rearrange("p (h d) -> p h d", h=NH), rot.unsqueeze(1).to_broadcast([P, NH, ROPE]), per_head(1, ROPE), ALU.mult).then_inc(tok_ready, 1)

            for c in range(TT * IH // 2):
                b, pr = c // (IH // 2), c % (IH // 2)
                S = P * (b + 1)
                acc = work[b][:, 0:S]
                dve.wait_ge(relu_done, c + 1)
                for r in range(2):
                    h = 2 * pr + r
                    w = proj[b][:, O_WI + h:O_WI + h + 1]
                    dot = relu_buf[c % 2][:, r * S:r * S + S]
                    if h == 0:
                        link(V.tensor_scalar(acc, dot, w, None, ALU.mult))
                    else:
                        link(V.scalar_tensor_tensor(acc, dot, w, acc, ALU.mult, ALU.add))
                V.tensor_copy(top8, relu_buf[c % 2][:, 0:8]).then_inc(acc_done, 1)
            dve.wait_ge(acc_done, TT * IH // 2)
            dve.wait_ge(bias_in, 32)
            for b in range(TT):
                S = P * (b + 1)
                left = work[b][:, 0:S]
                link(V.tensor_tensor(left, left, chunk_mask[:, b, 0:S], ALU.add))
                for _ in range(N_SEL // 8):
                    link(V.max(top8, left))
                    link(V.match_replace(left, top8, left, REMOVED))
                link(V.tensor_scalar(left, left, REMOVED / 2, MASKED, ALU.is_gt, ALU.mult))
                link(V.tensor_tensor(bias[b][:, :, 0:S], bias[b][:, :, 0:S], left.unsqueeze(1).to_broadcast([P, NH, S]), ALU.add))

            def logits(j):
                g, pr, b = JOBS[j]
                S = P * (b + 1)
                dve.wait_ge(logit_mm, j + 1)
                if j >= 2:
                    dve.wait_ge(pT_mm, j - 1)
                ops = []
                for hh in range(2):
                    h = 2 * pr + hh
                    add = bias[b][:, h, 0:S] if g else chunk_mask[:, b, 0:S]
                    ops.append(V.scalar_tensor_tensor(logit[j % 2][:, hh * S:hh * S + S], ps[:, j % 2, hh * S:hh * S + S],
                                                      rs_h[:, b, 2 * g, h:h + 1], add, ALU.mult, ALU.add))
                link(*ops)
                V.tensor_reduce(j_nmax[:, 2 * j:2 * j + 2], logit[j % 2][:, 0:2 * S].rearrange("p (h s) -> p h s", h=2), AX, ALU.max, negate=True).then_inc(logit_done, 1)

            def normalise(j):
                S = P * (JOBS[j][2] + 1)
                dve.wait_ge(exp_done, j + 1)
                link(V.reciprocal(j_rec[:, 2 * j:2 * j + 2], j_sum[:, 2 * j:2 * j + 2]))
                for hh in range(2):
                    part = logit[j % 2][:, hh * S:hh * S + S]
                    ins = V.tensor_scalar(part, part, j_rec[:, 2 * j + hh:2 * j + hh + 1], None, ALU.mult)
                ins.then_inc(prob_done, 1)

            def y_lo(j):
                g, pr, b = JOBS[j]
                k = g * NH + 2 * pr
                dve.wait_ge(yhi_done, j + 1)
                V.tensor_tensor(hT_lo[:, k:k + 2, b * P:b * P + P], ps[:, 4 + j % 2, 0:256].rearrange("p (h t) -> p h t", h=2),
                                hT_hi[:, k:k + 2, b * P:b * P + P].bitcast(F32), ALU.subtract).then_inc(ylo_done, 1)
            for step in range(len(JOBS) + 2):
                if step < len(JOBS):
                    logits(step)
                if 1 <= step <= len(JOBS):
                    normalise(step - 1)
                if step >= 2:
                    y_lo(step - 2)

            def residual(n):
                dve.wait_ge(unit_used, B_WO + 8 * n + 8)
                for b in range(TT):
                    cols = xs[b][:, n * 512:n * 512 + 512]
                    V.tensor_tensor(cols, ps[:, 2 * (n % 2) + b, :], cols, ALU.add).then_inc(x2_done, 1)
            for n in range(D // 512):
                for j in range(8):
                    split_lo(B_WO + 8 * n + j, j)
                    if j == 1 and n:
                        if n == 1:
                            dve.wait_ge(x_back, 16)
                        residual(n - 1)
            residual(D // 512 - 1)

            norm_scale(1)
            norm_lo(1, G_FFN)
            with dve.Fori(0, U_PQ // 4) as i:
                for j in range(4):
                    split_lo(i * 4 + (B_PQ + j), j)

            for b in range(TT):
                for g in range(4):
                    dve.wait_ge(score_done, 4 * b + g + 1)
                sc = score[b]
                link(*[V.max(top_v[:, c, 0:8], sc[:, c, :]) for c in range(16)])
                link(*[V.max_index(top_iu[:, c, 0:8], top_v[:, c, 0:8], sc[:, c, :]) for c in range(16)])
                link(*[V.match_replace(sc[:, c, :], top_v[:, c, 0:8], sc[:, c, :], REMOVED) for c in range(16)])
                link(*[V.max(top_v[:, c, 8:16], sc[:, c, :]) for c in range(16)])
                link(*[V.max_index(top_iu[:, c, 8:16], top_v[:, c, 8:16], sc[:, c, :]) for c in range(16)])
                halves = top_v.rearrange("p (h f) j -> p h f j", f=2)
                link(V.tensor_copy(top_i, top_iu),
                     V.tensor_tensor(cand.rearrange("p (h i j) -> p h i j", h=NH, i=TOPK),
                                     halves[:, :, 0, :].unsqueeze(3).to_broadcast([P, NH, TOPK, TOPK]),
                                     halves[:, :, 1, :].unsqueeze(2).to_broadcast([P, NH, TOPK, TOPK]), ALU.add))
                pairs = [cand[:, 256 * h:256 * h + 256] for h in range(NH)]
                link(*[V.max(c_v[:, h, 0:8], pairs[h]) for h in range(NH)])
                link(*[V.max_index(c_iu[:, h, 0:8], c_v[:, h, 0:8], pairs[h]) for h in range(NH)])
                link(*[V.match_replace(pairs[h], c_v[:, h, 0:8], pairs[h], REMOVED) for h in range(NH)])
                link(*[V.max(c_v[:, h, 8:16], pairs[h]) for h in range(NH)])
                link(*[V.max_index(c_iu[:, h, 8:16], c_v[:, h, 8:16], pairs[h]) for h in range(NH)])
                if b:
                    dve.wait_ge(slotT_mm, b)
                link(V.tensor_scalar(c_digit_u[:, 0], c_iu, 4, None, ALU.logical_shift_right),
                     V.tensor_scalar(c_digit_u[:, 1], c_iu, 15, None, ALU.bitwise_and))
                link(V.tensor_copy(c_digit, c_digit_u))
                V.tensor_tensor(slot[:, 2, :].rearrange("p (h j) -> p h j", h=NH), c_v, c_v[:, :, 0:1].to_broadcast([P, NH, TOPK]), ALU.subtract).then_inc(cmax_done, 1)
                pick4 = pick.rearrange("p (h k j) -> p h k j", h=NH, k=TOPK)
                keys = top_i.rearrange("p (h f) j -> p h f j", f=2)
                for f in range(2):
                    link(V.tensor_tensor(pick4, c_digit[:, f].unsqueeze(3).to_broadcast([P, NH, TOPK, TOPK]),
                                         iota[:, 0:TOPK].unsqueeze(1).unsqueeze(1).to_broadcast([P, NH, TOPK, TOPK]), ALU.is_equal))
                    link(V.tensor_tensor(pick4, pick4, keys[:, :, f, :].unsqueeze(2).to_broadcast([P, NH, TOPK, TOPK]), ALU.mult))
                    link(V.tensor_reduce(slot[:, f, :], pick.rearrange("p (s j) -> p s j", j=TOPK), AX, ALU.add))
                dve.wait_ge(cexp_done, b + 1)
                gates = slot[:, 2, :].rearrange("p (h j) -> p h j", h=NH)
                link(V.tensor_reduce(gate_sum[:, 0:NH], gates, AX, ALU.add))
                link(V.reciprocal(gate_sum[:, NH:2 * NH], gate_sum[:, 0:NH]))
                V.tensor_tensor(gates, gates, gate_sum[:, NH:2 * NH].unsqueeze(2).to_broadcast([P, NH, TOPK]), ALU.mult).then_inc(slot_done, 1)
            for b in range(TT):
                dve.wait_ge(slotT_mm, b + 1)
                V.tensor_copy(slotT[:, :, b * P:b * P + P], ps[:, 6 + b, 0:384].rearrange("p (f t) -> p f t", f=3)).then_inc(slotT_done, 1)
            dve.wait_ge(slotT_done, TT)

            with dve.Fori(0, NKEY // 2) as i:
                for j in range(4):
                    split_lo(i * 4 + (B_U + j), j)

            def hots(g):
                for k in range(4):
                    t = g * 4 + k
                    if not (isinstance(g, int) and g == 0):
                        dve.wait_ge(gate_mm, g * 4 + (k - 3))
                    V.tensor_scalar(hot1[k], iota[:, :], slotT_flat[:, ds(g * 4 + (k + SEQ), 1)], None, ALU.is_equal)
                    V.tensor_scalar(hot0[k], iota[:, :], slotT_flat[:, ds(g * 4 + k, 1)], slotT_flat[:, ds(g * 4 + (k + 2 * SEQ), 1)],
                                    ALU.is_equal, ALU.mult).then_inc(hot_done, 1)

            def gate(g, par):
                dve.wait_ge(gate_mm, g * 4 + 4)
                a = acts_e[:, :, ds(g * 4, 4)].rearrange("p e t -> p t e")
                V.tensor_tensor(a, a, ps[:, 2 + par, :].rearrange("p (t e) -> p t e", t=4), ALU.mult).then_inc(gated, 1)
            slotT_flat = slotT[:, :, :].rearrange("p f t -> p (f t)")
            dve.wait_ge(gelu_done, NKEY)
            hots(0)
            hots(1)
            gate(0, 0)
            with dve.Fori(1, SEQ // 8) as i:
                hots(i * 2)
                gate(i * 2 - 1, 1)
                hots(i * 2 + 1)
                gate(i * 2, 0)
            gate(SEQ // 4 - 1, 1)
            dve.wait_ge(gated, SEQ // 4)

            def expert_pair(i):
                for j in range(4):
                    if j % 2 == 0:
                        dve.wait_ge(ehi_done, i * 2 + (j // 2 + 1))
                        V.tensor_tensor(elo[j // 2][:, :], acts[:, ds(i * (2 * SEQ) + (j // 2) * SEQ, SEQ)], ehi[j // 2][:, :].bitcast(F32),
                                        ALU.subtract).then_inc(elo_done, 1)
                    split_lo(i * 4 + (B_V + j), j)
            with dve.Fori(0, NKEY // 2) as i:
                expert_pair(i)
            dve.wait_ge(x2_back, 16)
            dve.wait_ge(unit_used, B_END)
            for g in range(8):
                b, n = g // 4, g % 4
                V.tensor_tensor(xn[b][:, n * 512:n * 512 + 512], ps[:, g, :], xs[b][:, n * 512:n * 512 + 512], ALU.add).then_inc(out_ready, 1)

        @block.tensor
        def _(pe):
            mm = nc.tensor.matmul

            pe.wait_ge(hot_in, 32)
            mm(ps[0:8, 7, :], acts[0:32, A_BIAS + 512:A_BIAS + 520], acts[0:32, A_BIAS:A_BIAS + 512], start=True, stop=True).then_inc(vec_mm, 1)

            def norm_transpose(nth):
                pe.wait_ge(xn_done, TT * nth + TT)
                for k in range(KD):
                    if k == 7 and nth == 0:
                        pe.wait_ge(vec_ready, 1)
                    if k >= 8:
                        pe.wait_ge(hTlo_done, nth * KD + k - 7)
                    for b in range(TT):
                        ins = nc.tensor.transpose(ps[:, k % 8, b * P:b * P + P], xn[b][:, k * P:k * P + P], ident[:, :])
                    ins.then_inc(xT_mm, 1)

            pe.wait_ge(const_in, 16)
            norm_transpose(0)

            def tall_block(base, n, par, w):
                for j in range(8):
                    pe.wait_ge(lo_done, n * 8 + (base + j + 1))
                    for kk in range(2):
                        k = 2 * j + kk
                        rows = slice(kk * w, kk * w + w)
                        for b in range(TT):
                            out = ps[:, 2 * par + b, 0:w]
                            t = slice(b * P, b * P + P)
                            mm(out, hT_hi[:, k, t], whi[j % NPART][:, rows], start=k == 0, stop=False)
                            mm(out, hT_hi[:, k, t], wlo[j % NPART][:, rows], start=False, stop=False)
                            ins = mm(out, hT_lo[:, k, t], whi[j % NPART][:, rows], start=False, stop=k == KD - 1)
                    ins.then_inc(unit_used, 1)

            pe.wait_ge(hTlo_done, KD)
            tall_block(0, 0, 0, 512)
            tall_block(0, 1, 1, 512)
            with pe.Fori(1, N_IN // 2 - 1) as i:
                for par in range(2):
                    pe.wait_ge(proj_done, i * 2 + (par - 1))
                    tall_block(0, i * 2 + par, par, 512)
            for n in (N_IN - 2, N_IN - 1):
                pe.wait_ge(proj_done, n - 1)
                tall_block(0, n, n % 2, width(n))

            pe.wait_ge(cn_done, 2 * TT)
            for k in range(6):
                off = O_CQ + P * k if k < 4 else O_CKV + P * (k - 4)
                for b in range(TT):
                    ins = nc.tensor.transpose(ps[:, k, b * P:b * P + P], proj[b][:, off:off + P], ident[:, :])
                ins.then_inc(cT_mm, 1)
            pe.wait_ge(cT_done, 6)
            pe.wait_ge(wu_in, 32)
            for g in range(14):
                b, n = g // 7, g % 7
                if g >= 8:
                    pe.wait_ge(up_done, g - 7)
                src, w, ks = (cqT, w_uq[:, :, n * 512:n * 512 + 512], 4) if n < 3 else (ckvT, w_ukv[:, :, (n - 3) * 512:(n - 3) * 512 + 512], 2)
                for k in range(ks):
                    ins = mm(ps[:, g % 8, :], src[:, k, b * P:b * P + P], w[:, k, :], start=k == 0, stop=k == ks - 1)
                ins.then_inc(up_mm, 1)

            pe.wait_ge(h_root, 4)
            for g, (srcs, dst, gain, need) in enumerate(GROUPS):
                pe.wait_ge(tok_ready, need)
                if g >= 8:
                    pe.wait_ge(headT_done, g - 7)
                for i, src in enumerate(srcs):
                    ins = nc.tensor.transpose(ps[:, g % 8, i * P:i * P + P], src, ident[:, :])
                ins.then_inc(headT_mm, 1)

            pe.wait_ge(headT_done, len(GROUPS))
            for c in range(TT * IH // 2):
                b, pr = c // (IH // 2), c % (IH // 2)
                S = P * (b + 1)
                if c >= 2:
                    pe.wait_ge(relu_done, c - 1)
                for r in range(2):
                    ins = mm(ps[:, 6 + c % 2, r * S:r * S + S], qiT[:, pr, b * P:b * P + P], kiT[:, r, 0:S], start=True, stop=True)
                ins.then_inc(dot_mm, 1)

            def products(j):
                g, pr, b = JOBS[j]
                S = P * (b + 1)
                t = slice(b * P, b * P + P)
                if j >= 2:
                    pe.wait_ge(logit_done, j - 1)
                for hh in range(2):
                    h = 2 * pr + hh
                    out = ps[:, j % 2, hh * S:hh * S + S]
                    if g == 0:
                        mm(out, qTn[:, h, t], kTn[:, h, 0:S], start=True, stop=False)
                        ins = mm(out, qTr[:, h, t], kTr[:, pr, 0:S], start=False, stop=True)
                    else:
                        ins = mm(out, qdT[:, h, t], kdT[:, h, 0:S], start=True, stop=True)
                ins.then_inc(logit_mm, 1)

            def prob_transpose(j):
                b = JOBS[j][2]
                pe.wait_ge(prob_done, j + 1)
                if j >= 2:
                    pe.wait_ge(pT_done, j - 1)
                for i in range(2 * (b + 1)):
                    ins = nc.tensor.transpose(ps[:, 2 + j % 2, i * P:i * P + P], logit[j % 2][:, i * P:i * P + P], ident[:, :])
                ins.then_inc(pT_mm, 1)

            def values(j):
                g, pr, b = JOBS[j]
                pe.wait_ge(pT_done, j + 1)
                if j >= 2:
                    pe.wait_ge(ylo_done, j - 1)
                for hh in range(2):
                    h = 2 * pr + hh
                    for s in range(b + 1):
                        v = proj[s][:, O_VD + h * HD:O_VD + h * HD + HD] if g else kv_h[s][:, h, NOPE:NOPE + HD]
                        i = hh * (b + 1) + s
                        ins = mm(ps[:, 4 + j % 2, hh * P:hh * P + P], v, probT[j % 2][:, i * P:i * P + P], start=s == 0, stop=s == b)
                ins.then_inc(y_mm, 1)
            for step in range(len(JOBS) + 2):
                if step < len(JOBS):
                    products(step)
                if 1 <= step <= len(JOBS):
                    prob_transpose(step - 1)
                if step >= 2:
                    values(step - 2)

            pe.wait_ge(ylo_done, len(JOBS))
            tall_block(B_WO, 0, 0, 512)
            tall_block(B_WO, 1, 1, 512)
            for n in (2, 3):
                pe.wait_ge(x2_done, TT * (n - 1))
                tall_block(B_WO, n, n % 2, 512)
            pe.wait_ge(x2_done, 8)
            norm_transpose(1)

            def wide_pair(i, base, out_done):
                for c in range(2):
                    if not (isinstance(i, int) and i == 0):
                        pe.wait_ge(out_done, i * 2 + (c - 1))
                    for half in range(2):
                        j = 2 * c + half
                        pe.wait_ge(lo_done, i * 4 + (base + j + 1))
                        for kk in range(8):
                            k = 8 * half + kk
                            w = slice(kk * P, kk * P + P)
                            out = ps[:, c, 0:SEQ]
                            mm(out, whi[half][:, w], hT_hi[:, k, :], start=k == 0, stop=False)
                            mm(out, whi[half][:, w], hT_lo[:, k, :], start=False, stop=False)
                            ins = mm(out, wlo[half][:, w], hT_hi[:, k, :], start=False, stop=k == KD - 1)
                        ins.then_inc(unit_used, 1)

            pe.wait_ge(hTlo_done, 2 * KD)
            wide_pair(0, B_PQ, qr_done)
            with pe.Fori(1, U_PQ // 4) as i:
                wide_pair(i, B_PQ, qr_done)
            pe.wait_ge(qr_done, 16)
            pe.wait_ge(subk_in, 16)
            for g in range(8):
                b, q = g // 4, g % 4
                if g >= 4:
                    pe.wait_ge(score_done, g - 3)
                for i in range(4):
                    c = 4 * q + i
                    ins = mm(ps[:, 2 + g % 4, i * P:i * P + P], qr[:, c, b * P:b * P + P], subk[:, c, :], start=True, stop=True)
                ins.then_inc(score_mm, 1)
            for b in range(TT):
                pe.wait_ge(slot_done, b + 1)
                for f in range(3):
                    ins = nc.tensor.transpose(ps[:, 6 + b, f * P:f * P + P], slot[:, f, :], ident[:, :])
                ins.then_inc(slotT_mm, 1)
            wide_pair(0, B_U, gelu_done)
            with pe.Fori(1, NKEY // 2) as i:
                wide_pair(i, B_U, gelu_done)
            def gate_pair(i):
                for q in range(2):
                    if not (isinstance(i, int) and i == 0):
                        pe.wait_ge(gated, i * 2 + (q - 1))
                    for k in range(4):
                        pe.wait_ge(hot_done, i * 8 + (4 * q + k + 1))
                        mm(ps[:, 2 + q, k * P:k * P + P], hot1[k], hot0[k], start=True, stop=True).then_inc(gate_mm, 1)
            gate_pair(0)
            with pe.Fori(1, SEQ // 8) as i:
                gate_pair(i)

            def expert_pair(i, first, last):
                for c in range(2):
                    pe.wait_ge(elo_done, i * 2 + (c + 1))
                    for half in range(2):
                        pe.wait_ge(lo_done, i * 4 + (B_V + 2 * c + half + 1))
                        start, stop = first and c == 0, last and c == 1
                        for b in range(TT):
                            t = slice(b * P, b * P + P)
                            for q in range(2):
                                out, cols = ps[:, 4 * b + 2 * half + q, :], slice(512 * q, 512 * q + 512)
                                mm(out, ehi[c][:, t], whi[half][:, cols], start=start, stop=False)
                                mm(out, ehi[c][:, t], wlo[half][:, cols], start=False, stop=False)
                            for q in range(2):
                                out, cols = ps[:, 4 * b + 2 * half + q, :], slice(512 * q, 512 * q + 512)
                                ins = mm(out, elo[c][:, t], whi[half][:, cols], start=False, stop=stop)
                        ins.then_inc(unit_used, 1)
            expert_pair(0, True, False)
            with pe.Fori(1, NKEY // 2 - 1) as i:
                expert_pair(i, False, False)
            expert_pair(NKEY // 2 - 1, False, True)

    return nc


def t5_bucket_of_distance(rel):
    n = np.abs(rel)
    nf = np.maximum(n, 1).astype(np.float32)
    large = 8 + (np.log(nf / np.float32(8)) / np.float32(math.log(16)) * np.float32(8)).astype(np.int32)
    return np.where(rel > 0, 16, 0) + np.where(n < 8, n, np.minimum(large, 15))


def shape_constants(seq):
    half, chunk, tiles = 32, 64, seq // 128
    pos = np.arange(seq)
    freqs = np.float32(10000.0) ** (np.float32(-2.0) * np.arange(half, dtype=np.float32) / np.float32(2 * half))
    ang = pos.astype(np.float32)[:, None] * freqs[None, :]
    rope = np.stack([np.cos(ang), np.sin(ang)]).reshape(2, tiles, 128, half).transpose(2, 0, 1, 3).reshape(128, -1)
    mask = np.where(pos[None, :] // chunk <= pos[:, None] // chunk, 0.0, -1.0e30)
    mask = mask.reshape(tiles, 128, seq).transpose(1, 0, 2).reshape(128, -1)
    distance = np.arange(512) - (seq - 1)
    hot = np.arange(32)[:, None] == t5_bucket_of_distance(distance)[None, :]
    made = {
        "ident": np.eye(128), "iota": np.tile(np.arange(128), (128, 1)), "eps": np.full((128, 1), 1e-6),
        "rope_tab": rope, "chunk_mask": mask, "bucket_hot": hot,
    }
    return {n: np.ascontiguousarray(a, dtype=np.float32) for n, a in made.items()}


def kernel(**inputs):
    import concourse.bacc as _bacc
    from concourse import mybir as _mybir
    from concourse.bass_utils import run_bass_kernel_spmd as _run

    a = {n: np.asarray(v) for n, v in inputs.items()}
    seq, d = a["x"].shape[1:]
    columns = lambda g: g.reshape(-1, 128).T
    sent = {
        "x": a["x"][0], "w_in": a["w_in"][0], "w_uq": a["w_uq"][0], "w_ukv": a["w_ukv"][0], "w_o": a["w_o"][0],
        "rel_bias": a["rel_bias"], "v_tab": a["v_tab"][0],
        "gains": np.concatenate([columns(a["g_attn"]), columns(a["g_ffn"]), columns(a["g_cq"]), columns(a["g_ckv"]),
                                 columns(a["g_mla_q"][:, 0:128]), columns(a["g_mla_k"][:, 0:128]), columns(a["g_dsa_q"]), columns(a["g_dsa_k"])], axis=1),
        "rope_gain": np.concatenate([a["g_mla_q"][:, 128:], a["g_mla_k"][:, 128:]], axis=1),
        "w_pq": a["w_pq"][0].reshape(2, 8, 128, 16, 128).transpose(3, 0, 2, 1, 4).reshape(-1, 1024),
        "u_tab": a["u_tab"][0].reshape(128, 128, 2, 8, 128).transpose(0, 2, 4, 3, 1).reshape(-1, 1024),
        "sub_keys": a["sub_keys"][0].reshape(16, 128, 128).transpose(2, 0, 1),
    }
    arrays = {f"in_{n}": np.ascontiguousarray(v) for n, v in {**sent, **shape_constants(seq)}.items()}
    nc = _bacc.Bacc("TRN2", target_bir_lowering=False, num_devices=1)
    f32 = _mybir.dt.float32
    io = {n[3:]: nc.dram_tensor(n, v.shape, _mybir.dt.from_np(v.dtype), kind="ExternalInput").ap() for n, v in arrays.items()}
    io["out"] = nc.dram_tensor("out_0", (seq, d), f32, kind="ExternalOutput").ap()
    io["x2_scratch"] = nc.dram_tensor("x2_scratch", (seq, d), f32, kind="Internal").ap()
    io["bias_scratch"] = nc.dram_tensor("bias_scratch", (8, 128, 512), f32, kind="Internal").ap()
    build_block(nc, io)
    r = _run(nc, [arrays], core_ids=[0])
    return r.results[0]["out_0"].reshape(1, seq, d)
```

```python
import math
from contextlib import ExitStack

import concourse.bass as bass
import numpy as np
from concourse import mybir


def build_block(nc, io):
    F32 = mybir.dt.float32
    F32R = mybir.dt.float32r
    U32 = mybir.dt.uint32
    ALU = mybir.AluOpType
    ACT = mybir.ActivationFunctionType
    AX = mybir.AxisListType.X
    ds = bass.ds

    P = 128
    SEQ, D = io["x"].shape
    TT = SEQ // P
    KD = D // P
    IN_W = io["w_in"].shape[1]
    QL, CKV, ROPE = 512, 256, 64
    NH, NOPE, HD = 8, 128, 128
    QK = NOPE + ROPE
    IH, ID = 16, 64
    N_SEL = SEQ // 4
    TOPK, NKEY = 16, 128
    EPS = 1e-6
    MASKED, REMOVED = -1.0e30, -3.0e38
    O_CQ, O_CKV, O_KR = 0, QL, QL + CKV
    O_QD = O_KR + ROPE
    O_KD = O_QD + NH * HD
    O_VD = O_KD + NH * HD
    O_QI = O_VD + NH * HD
    O_KI = O_QI + IH * ID
    O_WI = O_KI + ID
    assert O_WI + IH == IN_W

    UNIT = 1024
    PIECE = UNIT // 2
    NRAW, NPART = 4, 4
    N_IN = -(-IN_W // 512)
    LAST_W = IN_W - 512 * (N_IN - 1)
    U_IN, U_WO, U_PQ = 8 * N_IN, 8 * (D // 512), 2 * 16
    B_IN = 0
    B_WO = B_IN + U_IN
    B_PQ = B_WO + U_WO
    B_U = B_PQ + U_PQ
    B_V = B_U + 2 * NKEY
    B_END = B_V + 2 * NKEY

    with ExitStack() as ctx:
        def sb(name, shape, dt=F32):
            return ctx.enter_context(nc.sbuf_tensor(name, shape, dt))

        def sem(name):
            return ctx.enter_context(nc.semaphore(name))

        acts = sb("acts", [P, NKEY * SEQ])
        hT_hi = sb("hT_hi", [P, KD, SEQ], F32R)
        hT_lo = sb("hT_lo", [P, KD, SEQ], F32R)
        raw = [sb(f"raw{i}", [P, UNIT]) for i in range(NRAW)]
        whi = [sb(f"w_hi{i}", [P, PIECE], F32R) for i in range(NPART)]
        wlo = [sb(f"w_lo{i}", [P, PIECE], F32R) for i in range(NPART)]
        ehi = [sb(f"e_hi{i}", [P, SEQ], F32R) for i in range(2)]
        elo = [sb(f"e_lo{i}", [P, SEQ], F32R) for i in range(2)]
        ident = sb("ident", [P, P])
        iota = sb("iota", [P, P])
        eps = sb("eps", [P, 1])
        gains = sb("gains", [P, 2 * KD + 10])
        slotT = sb("slotT", [P, 3, SEQ])
        early = sb("early", [P, 1536])
        stat = sb("stat", [P, 288])
        ps = ctx.enter_context(nc.psum_tensor("ps", [P, 8, 512], F32))

        G_ATTN, G_FFN, G_CQ, G_CKV, G_MQ, G_MK, G_DQ, G_DK = 0, KD, 2 * KD, 2 * KD + 4, 2 * KD + 6, 2 * KD + 7, 2 * KD + 8, 2 * KD + 9

        ckvT = early[:, 0:512].rearrange("p (k t) -> p k t", k=2)
        chunk_mask = early[:, 512:1024].rearrange("p (b s) -> p b s", b=TT)
        kpad = early[:, 1024:1280].rearrange("p (r d) -> p r d", r=2)
        rope_tab = early[:, 1280:1408].rearrange("p (f b c) -> p f b c", f=2, b=TT)
        rope_gain = early[:, 1408:1536].rearrange("p (f c) -> p f c", f=2)
        krot = early[:, 0:512]
        hot1 = [early[:, 128 * i:128 * i + 128] for i in range(4)]
        hot0 = [early[:, 512 + 128 * i:512 + 128 * i + 128] for i in range(4)]
        gelu_buf = [early[:, 1024 + SEQ * i:1024 + SEQ * i + SEQ] for i in range(2)]

        def region(at, n):
            return acts[:, at:at + n]

        proj = [region(b * IN_W, IN_W) for b in range(TT)]
        A_WU = TT * IN_W
        w_uq = region(A_WU, 6144).rearrange("p (k n) -> p k n", k=4)
        w_ukv = region(A_WU + 6144, 4096).rearrange("p (k n) -> p k n", k=2)
        head_view = lambda at, n=8: region(at, n * SEQ).rearrange("p (h t) -> p h t", h=n)
        qTn, qTr, kTn = head_view(A_WU), head_view(A_WU + 2048), head_view(A_WU + 4096)
        kTr = head_view(A_WU + 6144, 4)
        qiT = head_view(A_WU + 7168)
        kiT = head_view(A_WU + 9216, 2)
        A_KV = A_WU + 10240
        kv = [region(A_KV + 2048 * b, 2048) for b in range(TT)]
        A_BIAS = A_KV + 4096
        bias = [region(A_BIAS + 2048 * b, 2048).rearrange("p (h s) -> p h s", h=NH) for b in range(TT)]
        A_QM = A_BIAS + 4096
        qm = [region(A_QM + 1536 * b, 1536) for b in range(TT)]
        A_TAIL = A_QM + 3072
        cqT = region(A_TAIL, 1024).rearrange("p (k t) -> p k t", k=4)
        qpad = region(A_TAIL, 1024)
        qdT, kdT = head_view(A_QM), head_view(A_QM + 2048)
        assert A_TAIL + 1024 <= NKEY * SEQ
        rope_tmp = [proj[0][:, 256 * i:256 * i + 256] for i in range(3)] + [proj[1][:, 0:256], proj[1][:, 256:320]]
        relu_buf = [proj[0][:, O_QD + 512 * i:O_QD + 512 * i + 512] for i in range(2)]
        work = [proj[1][:, O_QD + 256 * b:O_QD + 256 * b + 256] for b in range(TT)]
        logit = [proj[0][:, O_KD + 512 * i:O_KD + 512 * i + 512] for i in range(2)]
        probT = [proj[1][:, O_KD + 512 * i:O_KD + 512 * i + 512] for i in range(2)]
        bias_vec = region(A_WU, 512)
        xs = [region(D * b, D) for b in range(TT)]
        xn = [region(TT * D + D * b, D) for b in range(TT)]
        qr = region(2 * TT * D, 16 * SEQ).rearrange("p (c t) -> p c t", c=16)
        subk = region(2 * TT * D + 16 * SEQ, 16 * NKEY).rearrange("p (c n) -> p c n", c=16)
        A_SCORE = NKEY * SEQ - TT * 2048
        A_TK = A_SCORE - 2560
        score = [region(A_SCORE + 2048 * b, 2048).rearrange("p (c n) -> p c n", c=16) for b in range(TT)]
        A_SLOT = A_TK
        slot = region(A_SLOT, 3 * SEQ).rearrange("p (f s) -> p f s", f=3)
        h_score = region(A_TK + 768, 256).rearrange("p (f n) -> p f n", f=2)
        cand = region(A_TK + 1024, 256)
        pick = region(A_TK + 1280, 512).rearrange("p (f k j) -> p f k j", f=2, k=TOPK)
        pair16 = lambda at: region(A_TK + 1792 + at, 32).rearrange("p (f j) -> p f j", f=2)
        top_v, top_iu, top_i, c_digit_u, c_digit = pair16(0), pair16(32).bitcast(U32), pair16(64), pair16(96).bitcast(U32), pair16(128)
        c_v, c_iu = region(A_TK + 1952, 16), region(A_TK + 1968, 16).bitcast(U32)
        gate_sum = region(A_TK + 1984, 32).rearrange("p (f j) -> p f j", f=2)
        acts_e = acts[:, :].rearrange("p (e t) -> p e t", t=SEQ)

        ss_x, rs_x = stat[:, 0:2], stat[:, 2:4]
        ss_c, rs_c = stat[:, 4:8], stat[:, 8:12]
        ss_kr = stat[:, 12:14]
        ss_h = stat[:, 16:80].rearrange("p (b k h) -> p b k h", b=TT, k=4)
        rs_h = stat[:, 80:144].rearrange("p (b k h) -> p b k h", b=TT, k=4)
        j_max, j_nmax = stat[:, 144:176], stat[:, 176:208]
        j_sum, j_rec = stat[:, 208:240], stat[:, 240:272]
        top8 = stat[:, 272:280]
        carrier = stat[:, 280:281]

        raw_ready = [sem(f"raw_ready{i}") for i in range(NRAW)]
        hi_done, lo_done, piece_used = sem("hi_done"), sem("lo_done"), sem("piece_used")
        x_in, const_in, gain_in, mask_in, wu_in = sem("x_in"), sem("const_in"), sem("gain_in"), sem("mask_in"), sem("wu_in")
        hot_in, vec_mm, vec_ready, vec_out, bias_in = sem("hot_in"), sem("vec_mm"), sem("vec_ready"), sem("vec_out"), sem("bias_in")
        x_back, subk_in, x2_done, x2_stored, x2_back = sem("x_back"), sem("subk_in"), sem("x2_done"), sem("x2_stored"), sem("x2_back")
        x_root, xn_done, xT_mm, hThi_done, hTlo_done = sem("x_root"), sem("xn_done"), sem("xT_mm"), sem("hThi_done"), sem("hTlo_done")
        proj_done = sem("proj_done")
        c_root, cn_done, cT_mm, cT_done, up_mm, up_done = sem("c_root"), sem("cn_done"), sem("cT_mm"), sem("cT_done"), sem("up_mm"), sem("up_done")
        sq_done, red_done, ss_done, h_root = sem("sq_done"), sem("red_done"), sem("ss_done"), sem("h_root")
        tok_ready, headT_mm, headT_done = sem("tok_ready"), sem("headT_mm"), sem("headT_done")
        dot_mm, relu_done, acc_done = sem("dot_mm"), sem("relu_done"), sem("acc_done")
        logit_mm, logit_done, exp_done, prob_done = sem("logit_mm"), sem("logit_done"), sem("exp_done"), sem("prob_done")
        pT_mm, pT_done, y_mm, yhi_done, ylo_done = sem("pT_mm"), sem("pT_done"), sem("y_mm"), sem("yhi_done"), sem("ylo_done")
        qr_done, score_mm, score_done = sem("qr_done"), sem("score_mm"), sem("score_done")
        head_step, slot_ready, cexp_done, slot_done = sem("head_step"), sem("slot_ready"), sem("cexp_done"), sem("slot_done")
        slotT_mm, slotT_done, ones_set, applied = sem("slotT_mm"), sem("slotT_done"), sem("ones_set"), sem("applied")
        gelu_done, hot_done, gate_mm, gated = sem("gelu_done"), sem("hot_done"), sem("gate_mm"), sem("gated")
        ehi_done, elo_done, out_ready, out_sent = sem("ehi_done"), sem("elo_done"), sem("out_ready"), sem("out_sent")
        dve_chain, act_chain = sem("dve_chain"), sem("act_chain")

        JOBS = [(g, pr, b) for g in range(2) for pr in range(NH // 2) for b in range(TT)]
        kv_h = [kv[b].rearrange("p (h d) -> p h d", h=NH) for b in range(TT)]
        qm_h = [qm[b].rearrange("p (h d) -> p h d", h=NH) for b in range(TT)]

        def tile_groups():
            for b in range(TT):
                t = slice(b * P, b * P + P)
                for g in range(2):
                    yield [qm_h[b][:, 4 * g + i, 0:NOPE] for i in range(4)], qTn[:, 4 * g:4 * g + 4, t], G_MQ, 2 * b + 1
                for g in range(2):
                    yield [proj[b][:, O_QI + 128 * (4 * g + i):O_QI + 128 * (4 * g + i) + 128] for i in range(4)], qiT[:, 4 * g:4 * g + 4, t], None, 2 * b + 1
                yield [kpad[:, r, :] for r in range(2)], kiT[:, :, t], None, 2 * b + 1
                for g in range(2):
                    yield [kv_h[b][:, 4 * g + i, 0:NOPE] for i in range(4)], kTn[:, 4 * g:4 * g + 4, t], G_MK, 2 * b + 2
                yield [krot[:, 128 * i:128 * i + 128] for i in range(4)], kTr[:, :, t], None, 2 * b + 2
                for g in range(2):
                    yield [qpad[:, 128 * (4 * g + i):128 * (4 * g + i) + 128] for i in range(4)], qTr[:, 4 * g:4 * g + 4, t], None, 2 * b + 2
            for b in range(TT):
                t = slice(b * P, b * P + P)
                for off, dst, gain in ((O_QD, qdT, G_DQ), (O_KD, kdT, G_DK)):
                    for g in range(2):
                        yield [proj[b][:, off + 128 * (4 * g + i):off + 128 * (4 * g + i) + 128] for i in range(4)], dst[:, 4 * g:4 * g + 4, t], gain, 2 * TT
        GROUPS = list(tile_groups())
        GROUPS_OF_TILE = 10

        SQUARES = []
        for b, banks in enumerate(((0, 3, 5, 0), (2, 5, 0, 2))):
            SQUARES += [(qm_h[b], banks[0], 3, b, 0), (kv_h[b][:, :, 0:NOPE], banks[1], 2, b, 1),
                        (proj[b][:, O_QD:O_KD].rearrange("p (h d) -> p h d", h=NH), banks[2], 2, b, 2),
                        (proj[b][:, O_KD:O_VD].rearrange("p (h d) -> p h d", h=NH), banks[3], 2, b, 3)]

        block = ctx.enter_context(nc.Block())

        def width(n):
            return 512 if not isinstance(n, int) or n < N_IN - 1 else LAST_W

        @block.sync
        def _(sp):
            def load(u, j, src):
                if not (isinstance(u, int) and u < NRAW):
                    sp.wait_ge(lo_done, u * 2 - 2 * (NRAW - 1))
                dst = raw[j % NRAW][:, 0:src.free_size()]
                if len(src.shape) == 3:
                    dst = dst.rearrange("p (k n) -> p k n", k=src.shape[1])
                sp.dma_start(dst, src).then_inc(raw_ready[j % NRAW], 16)

            sp.dma_start(acts[:, 0:TT * D].rearrange("p (b d) -> p b d", b=TT), io["x"].rearrange("(b p) d -> p b d", p=P)).then_inc(x_in, 16)
            sp.dma_start(ident[:, :], io["ident"]).then_inc(const_in, 16)
            sp.dma_start(eps[:, :], io["eps"]).then_inc(gain_in, 16)
            sp.dma_start(gains[:, :], io["gains"]).then_inc(gain_in, 16)
            win = io["w_in"].rearrange("(k p) n -> p k n", p=P)
            for j in range(8):
                load(j, j, win[:, 2 * j:2 * j + 2, 0:512])
            with sp.Fori(1, N_IN - 1) as n:
                for j in range(8):
                    load(n * 8 + j, j, win[:, 2 * j:2 * j + 2, ds(n * 512, 512)])
            for j in range(8):
                load(B_IN + 8 * (N_IN - 1) + j, j, win[:, 2 * j:2 * j + 2, 512 * (N_IN - 1):IN_W])
            wo = io["w_o"].rearrange("(k p) n -> p k n", p=P)
            with sp.Fori(0, D // 512) as n:
                for j in range(8):
                    load(n * 8 + (B_WO + j), j, wo[:, 2 * j:2 * j + 2, ds(n * 512, 512)])
            with sp.Fori(0, U_PQ // 4) as i:
                for j in range(4):
                    load(i * 4 + (B_PQ + j), j, io["w_pq"][ds(i * (4 * P) + j * P, P), :])
            with sp.Fori(0, 2 * NKEY // 4) as i:
                for j in range(4):
                    load(i * 4 + (B_U + j), j, io["u_tab"][ds(i * (4 * P) + j * P, P), :])
            with sp.Fori(0, 2 * NKEY // 4) as i:
                for j in range(4):
                    load(i * 4 + (B_V + j), j,
                         io["v_tab"][ds(i * (2 * P) + (j // 2) * P, P), (j % 2) * UNIT:(j % 2) * UNIT + UNIT])
            for g in range(8):
                b, n = g // 4, g % 4
                sp.wait_ge(out_ready, g + 1)
                sp.dma_start(io["out"][b * P:b * P + P, n * 512:n * 512 + 512], xn[b][:, n * 512:n * 512 + 512]).then_inc(out_sent, 16)
            sp.wait_ge(out_sent, 16 * 8)
            sp.wait_ge(x2_stored, 16)
            sp.wait_ge(vec_out, 16)

        @block.gpsimd
        def _(pool):
            pool.dma_start(acts[0:32, A_BIAS:A_BIAS + 512], io["bucket_hot"]).then_inc(hot_in, 16)
            pool.dma_start(acts[0:32, A_BIAS + 512:A_BIAS + 520], io["rel_bias"]).then_inc(hot_in, 16)
            pool.dma_start(iota[:, :], io["iota"]).then_inc(mask_in, 16)
            pool.dma_start(early[:, 1280:1408], io["rope_tab"]).then_inc(mask_in, 16)
            pool.dma_start(early[:, 512:1024], io["chunk_mask"]).then_inc(mask_in, 16)
            pool.dma_start(early[:, 1408:1536], io["rope_gain"].to_broadcast([P, 128])).then_inc(mask_in, 16)
            pool.wait_ge(vec_ready, 1)
            pool.dma_start(io["bias_scratch"], acts[0:8, A_WU:A_WU + 512].unsqueeze(1).to_broadcast([8, P, 512])).then_inc(vec_out, 16)
            pool.wait_ge(vec_out, 16)
            for b in range(TT):
                first = SEQ - 1 - b * P
                src = bass.AP(io["bias_scratch"].tensor, first, [[511, P], [512 * P, NH], [1, SEQ]])
                pool.dma_start(bias[b], src).then_inc(bias_in, 16)
            pool.dma_start(w_uq, io["w_uq"].rearrange("(k p) n -> p k n", p=P)).then_inc(wu_in, 16)
            pool.dma_start(w_ukv, io["w_ukv"].rearrange("(k p) n -> p k n", p=P)).then_inc(wu_in, 16)
            pool.wait_ge(ylo_done, len(JOBS))
            pool.dma_start(acts[:, 0:TT * D].rearrange("p (b d) -> p b d", b=TT), io["x"].rearrange("(b p) d -> p b d", p=P)).then_inc(x_back, 16)
            pool.dma_start(subk, io["sub_keys"]).then_inc(subk_in, 16)
            pool.wait_ge(x2_done, 8)
            pool.dma_start(io["x2_scratch"].rearrange("(b p) d -> p b d", p=P), acts[:, 0:TT * D].rearrange("p (b d) -> p b d", b=TT)).then_inc(x2_stored, 16)
            pool.wait_ge(x2_stored, 16)
            half = NKEY * SEQ // 2
            pool.memset(region(half, A_TK - half), 1.0).then_inc(ones_set, 1)
            pool.wait_ge(slot_ready, NH)
            pool.memset(region(A_SCORE, 2048), 1.0).then_inc(ones_set, 1)
            pool.wait_ge(slotT_mm, TT)
            pool.memset(region(A_TK, 2560), 1.0)
            pool.memset(region(A_SCORE + 2048, 2048), 1.0).then_inc(ones_set, 1)
            pool.wait_ge(piece_used, 2 * B_V + 4 * (TT * D // SEQ))
            pool.dma_start(acts[:, 0:TT * D].rearrange("p (b d) -> p b d", b=TT), io["x2_scratch"].rearrange("(b p) d -> p b d", p=P)).then_inc(x2_back, 16)

        @block.scalar
        def _(act):
            links = [0]

            def link(*ins):
                for i in ins:
                    i.then_inc(act_chain, 1)
                links[0] += len(ins)
                act.wait_ge(act_chain, links[0])

            def split_hi(u, j, w=PIECE):
                act.wait_ge(raw_ready[j % NRAW], (u - j % NRAW) * (16 // NRAW) + 16)
                for half in range(2):
                    if not (isinstance(u, int) and 2 * u + half < NPART):
                        act.wait_ge(piece_used, u * 2 + (half + 1 - NPART))
                    nc.scalar.activation(whi[(2 * j + half) % NPART][:, 0:w], raw[j % NRAW][:, half * w:half * w + w], ACT.Copy).then_inc(hi_done, 1)

            def norm_root():
                link(*[nc.scalar.activation(xn[b], xs[b], ACT.Square, accum_out=ss_x[:, b:b + 1]) for b in range(TT)])
                nc.scalar.activation(rs_x, ss_x, ACT.Sqrt, bias=eps[:, :], scale=1.0 / D).then_inc(x_root, 1)

            def norm_hi(first, gain):
                for k in range(KD):
                    act.wait_ge(xT_mm, first + k + 1)
                    nc.scalar.activation(hT_hi[:, k, :], ps[:, k % 8, 0:SEQ], ACT.Copy,
                                         scale=gains[:, gain + k:gain + k + 1]).then_inc(hThi_done, 1)

            act.wait_ge(x_in, 16)
            act.wait_ge(gain_in, 32)
            norm_root()
            norm_hi(0, G_ATTN)

            def proj_out(n, par):
                act.wait_ge(piece_used, n * 16 + 16)
                for b in range(TT):
                    ins = nc.scalar.activation(acts[:, ds(n * 512 + b * IN_W, width(n))], ps[:, 2 * par + b, 0:width(n)], ACT.Copy)
                ins.then_inc(proj_done, 1)

            def in_block(n, par):
                for j in range(8):
                    split_hi(n * 8 + j, j, width(n))
                    if j == 1 and not (isinstance(n, int) and n == 0):
                        proj_out(n - 1, 1 - par)
            in_block(0, 0)
            in_block(1, 1)
            with act.Fori(1, N_IN // 2 - 1) as i:
                in_block(i * 2, 0)
                in_block(i * 2 + 1, 1)
            in_block(N_IN - 2, 0)
            in_block(N_IN - 1, 1)
            proj_out(N_IN - 1, 1)
            act.wait_ge(proj_done, N_IN)

            squares = []
            for b in range(TT):
                squares.append(nc.scalar.activation(ps[:, 4 + 2 * b, :], proj[b][:, O_CQ:O_CQ + QL], ACT.Square, accum_out=ss_c[:, b:b + 1]))
                squares.append(nc.scalar.activation(ps[:, 5 + 2 * b, 0:CKV], proj[b][:, O_CKV:O_CKV + CKV], ACT.Square, accum_out=ss_c[:, 2 + b:3 + b]))
            link(*squares)
            nc.scalar.activation(rs_c[:, 0:2], ss_c[:, 0:2], ACT.Sqrt, bias=eps[:, :], scale=1.0 / QL).then_inc(c_root, 1)
            nc.scalar.activation(rs_c[:, 2:4], ss_c[:, 2:4], ACT.Sqrt, bias=eps[:, :], scale=1.0 / CKV).then_inc(c_root, 1)
            for k in range(6):
                act.wait_ge(cT_mm, k + 1)
                dst, gain = (cqT[:, k, :], G_CQ + k) if k < 4 else (ckvT[:, k - 4, :], G_CKV + k - 4)
                nc.scalar.activation(dst, ps[:, k, 0:SEQ], ACT.Copy,
                                     scale=gains[:, gain:gain + 1]).then_inc(cT_done, 1)
            for g in range(14):
                b, n = g // 7, g % 7
                act.wait_ge(up_mm, g + 1)
                dst = qm[b][:, n * 512:n * 512 + 512] if n < 3 else kv[b][:, (n - 3) * 512:(n - 3) * 512 + 512]
                nc.scalar.activation(dst, ps[:, g % 8, :], ACT.Copy).then_inc(up_done, 1)
            act.wait_ge(up_done, 14)

            link(*[nc.scalar.activation(ps[:, 7, b * ROPE:b * ROPE + ROPE], proj[b][:, O_KR:O_KR + ROPE], ACT.Square, accum_out=ss_kr[:, b:b + 1]) for b in range(TT)])
            for i, (src, bank, banks, b, kind) in enumerate(SQUARES):
                if i >= 3:
                    act.wait_ge(red_done, i - 2)
                n = src.free_size()
                dst = ps[:, bank:bank + banks, :].rearrange("p a n -> p (a n)")[:, 0:n].rearrange("p (h d) -> p h d", h=NH)
                nc.scalar.activation(dst, src, ACT.Square).then_inc(sq_done, 1)
            act.wait_ge(ss_done, 2)
            for kind, n in ((0, QK), (1, QK), (2, HD), (3, HD)):
                nc.scalar.activation(rs_h[:, :, kind, :], ss_h[:, :, kind, :], ACT.Sqrt, bias=eps[:, :], scale=1.0 / n).then_inc(h_root, 1)

            for g, (srcs, dst, gain, _) in enumerate(GROUPS):
                act.wait_ge(headT_mm, g + 1)
                src = ps[:, g % 8, 0:128 * len(srcs)].rearrange("p (h t) -> p h t", t=P)
                scale = 1.0 if gain is None else gains[:, gain:gain + 1]
                nc.scalar.activation(dst, src, ACT.Copy, scale=scale).then_inc(headT_done, 1)

            for c in range(TT * IH // 2):
                S = P * (c // (IH // 2) + 1)
                act.wait_ge(dot_mm, c + 1)
                if c >= 2:
                    act.wait_ge(acc_done, c - 1)
                nc.scalar.activation(relu_buf[c % 2][:, 0:2 * S], ps[:, 6 + c % 2, 0:2 * S], ACT.Relu, scale=ID ** -0.5).then_inc(relu_done, 1)

            def exps(j):
                S = P * (JOBS[j][2] + 1)
                act.wait_ge(logit_done, j + 1)
                for hh in range(2):
                    part = logit[j % 2][:, hh * S:hh * S + S]
                    ins = nc.scalar.activation(part, part, ACT.Exp, bias=j_nmax[:, 2 * j + hh:2 * j + hh + 1],
                                               accum_out=j_sum[:, 2 * j + hh:2 * j + hh + 1])
                ins.then_inc(exp_done, 1)

            def probT_out(j):
                S = P * (JOBS[j][2] + 1)
                act.wait_ge(pT_mm, j + 1)
                if j >= 2:
                    act.wait_ge(y_mm, j - 1)
                nc.scalar.activation(probT[j % 2][:, 0:2 * S], ps[:, 2 + j % 2, 0:2 * S], ACT.Copy).then_inc(pT_done, 1)

            def y_hi(j):
                g, pr, b = JOBS[j]
                k = g * NH + 2 * pr
                act.wait_ge(y_mm, j + 1)
                nc.scalar.activation(hT_hi[:, k:k + 2, b * P:b * P + P], ps[:, 4 + j % 2, 0:256].rearrange("p (h t) -> p h t", h=2),
                                     ACT.Copy).then_inc(yhi_done, 1)
            for step in range(len(JOBS) + 2):
                if step < len(JOBS):
                    exps(step)
                if 1 <= step <= len(JOBS):
                    probT_out(step - 1)
                if step >= 2:
                    y_hi(step - 2)

            with act.Fori(0, U_WO // 4) as i:
                for j in range(4):
                    split_hi(i * 4 + (B_WO + j), j)

            act.wait_ge(x2_done, 8)
            norm_root()
            norm_hi(KD, G_FFN)

            def chunk_pair(i, base, out):
                for j in range(4):
                    split_hi(i * 4 + (base + j), j)
                    if j == 1 and not (isinstance(i, int) and i == 0):
                        out(i * 2 - 1, 1)
                    if j == 3:
                        out(i * 2, 0)

            def queries_out(c, par):
                act.wait_ge(piece_used, c * 4 + (2 * B_PQ + 4))
                nc.scalar.activation(acts[:, ds(c * SEQ + 2 * TT * D, SEQ)], ps[:, par, 0:SEQ], ACT.Copy).then_inc(qr_done, 1)

            chunk_pair(0, B_PQ, queries_out)
            with act.Fori(1, U_PQ // 4) as i:
                chunk_pair(i, B_PQ, queries_out)
            queries_out(15, 1)
            for g in range(8):
                b, q = g // 4, g % 4
                act.wait_ge(score_mm, g + 1)
                nc.scalar.activation(score[b][:, 4 * q:4 * q + 4, :], ps[:, 2 + g % 4, :].rearrange("p (c n) -> p c n", c=4), ACT.Copy).then_inc(score_done, 1)
            act.wait_ge(x2_stored, 16)

            def gelu(c, par):
                act.wait_ge(piece_used, c * 4 + (2 * B_U + 4))
                nc.scalar.activation(acts[:, ds(c * SEQ, SEQ)], ps[:, par, 0:SEQ], ACT.Gelu).then_inc(gelu_done, 1)
            chunk_pair(0, B_U, gelu)
            with act.Fori(1, NKEY // 4) as i:
                chunk_pair(i, B_U, gelu)
            gelu(NKEY // 2 - 1, 1)

            act.wait_ge(slot_ready, 2 * NH)
            nc.scalar.activation(slot[:, 2, :], slot[:, 2, :], ACT.Exp).then_inc(cexp_done, 1)

            def gelu_beside(c, par):
                act.wait_ge(piece_used, c * 4 + (2 * B_U + 4))
                if not (isinstance(c, int) and c < NKEY // 2 + 2):
                    act.wait_ge(applied, c - (NKEY // 2 + 1))
                nc.scalar.activation(gelu_buf[par], ps[:, par, 0:SEQ], ACT.Gelu).then_inc(gelu_done, 1)

            def second_half(i, first):
                for j in range(4):
                    split_hi(i * 4 + (B_U + j), j)
                    if j == 1 and not first:
                        gelu_beside(i * 2 - 1, 1)
                    if j == 3:
                        gelu_beside(i * 2, 0)
            second_half(NKEY // 4, True)
            second_half(NKEY // 4 + 1, False)
            with act.Fori(NKEY // 4 + 2, NKEY // 2) as i:
                second_half(i, False)
            gelu_beside(NKEY - 1, 1)

            act.wait_ge(gated, SEQ // 4)
            act.wait_ge(applied, NKEY // 2)

            def expert_pair(i):
                for j in range(4):
                    if j % 2 == 0:
                        if not (isinstance(i, int) and i == 0):
                            act.wait_ge(piece_used, i * 8 + (2 * B_V + 2 * j - 4))
                        nc.scalar.activation(ehi[j // 2][:, :], acts[:, ds(i * (2 * SEQ) + (j // 2) * SEQ, SEQ)], ACT.Copy).then_inc(ehi_done, 1)
                    split_hi(i * 4 + (B_V + j), j)
            expert_pair(0)
            with act.Fori(1, NKEY // 2) as i:
                expert_pair(i)

        @block.vector
        def _(dve):
            links = [0]
            V = nc.vector

            def link(*ins):
                for i in ins:
                    i.then_inc(dve_chain, 1)
                links[0] += len(ins)
                dve.wait_ge(dve_chain, links[0])

            def split_lo(u, j, w=PIECE):
                for half in range(2):
                    dve.wait_ge(hi_done, u * 2 + (half + 1))
                    slot_no = (2 * j + half) % NPART
                    V.tensor_tensor(wlo[slot_no][:, 0:w], raw[j % NRAW][:, half * w:half * w + w], whi[slot_no][:, 0:w].bitcast(F32),
                                    ALU.subtract).then_inc(lo_done, 1)

            def norm_scale(nth):
                dve.wait_ge(x_root, nth + 1)
                link(V.reciprocal(rs_x, rs_x))
                for b in range(TT):
                    V.tensor_scalar(xn[b], xs[b], rs_x[:, b:b + 1], None, ALU.mult).then_inc(xn_done, 1)

            def norm_lo(nth, gain):
                for k in range(KD):
                    dve.wait_ge(hThi_done, nth * KD + k + 1)
                    V.scalar_tensor_tensor(hT_lo[:, k, :], ps[:, k % 8, 0:SEQ], gains[:, gain + k:gain + k + 1],
                                           hT_hi[:, k, :].bitcast(F32), ALU.mult, ALU.subtract).then_inc(hTlo_done, 1)

            link(V.memset(kpad, 0.0))
            dve.wait_ge(vec_mm, 1)
            V.tensor_copy(acts[0:8, A_WU:A_WU + 512], ps[0:8, 7, :]).then_inc(vec_ready, 1)
            norm_scale(0)
            norm_lo(0, G_ATTN)

            with dve.Fori(0, (N_IN - 1) * 2) as i:
                for j in range(4):
                    split_lo(i * 4 + j, j)
            for j in range(8):
                split_lo(8 * (N_IN - 1) + j, j, LAST_W)

            dve.wait_ge(c_root, 2)
            link(V.reciprocal(rs_c, rs_c))
            for b in range(TT):
                V.tensor_scalar(proj[b][:, O_CQ:O_CQ + QL], proj[b][:, O_CQ:O_CQ + QL], rs_c[:, b:b + 1], None, ALU.mult).then_inc(cn_done, 1)
                V.tensor_scalar(proj[b][:, O_CKV:O_CKV + CKV], proj[b][:, O_CKV:O_CKV + CKV], rs_c[:, 2 + b:3 + b], None, ALU.mult).then_inc(cn_done, 1)

            for i, (src, bank, banks, b, kind) in enumerate(SQUARES):
                dve.wait_ge(sq_done, i + 1)
                n = src.free_size()
                sq = ps[:, bank:bank + banks, :].rearrange("p a n -> p (a n)")[:, 0:n].rearrange("p (h d) -> p h d", h=NH)
                V.tensor_reduce(ss_h[:, b, kind, :], sq, AX, ALU.add).then_inc(red_done, 1)
            dve.wait_ge(red_done, len(SQUARES))
            for b in range(TT):
                V.tensor_scalar(ss_h[:, b, 1, :], ss_h[:, b, 1, :], ss_kr[:, b:b + 1], None, ALU.add).then_inc(ss_done, 1)
            dve.wait_ge(h_root, 4)
            link(V.reciprocal(rs_h, rs_h))
            link(V.tensor_scalar(rs_h[:, :, 0, :], rs_h[:, :, 0, :], QK ** -0.5, None, ALU.mult),
                 V.tensor_scalar(rs_h[:, :, 2, :], rs_h[:, :, 2, :], HD ** -0.5, None, ALU.mult))

            dve.wait_ge(mask_in, 64)
            link(V.memset(qpad, 0.0))
            for b in range(TT):
                if b:
                    dve.wait_ge(headT_mm, 5)
                key = proj[b][:, O_KI:O_KI + ID]
                V.tensor_copy(kpad[:, 0, 0:ID], key)
                V.tensor_copy(kpad[:, 1, ID:2 * ID], key).then_inc(tok_ready, 1)
                def per_head(kind, n):
                    return rs_h[:, b, kind, :].unsqueeze(2).to_broadcast([P, NH, n])
                kn = kv_h[b][:, :, 0:NOPE]
                V.tensor_tensor(kn, kn, per_head(1, NOPE), ALU.mult)
                kd = proj[b][:, O_KD:O_VD].rearrange("p (h d) -> p h d", h=NH)
                V.tensor_tensor(kd, kd, per_head(3, HD), ALU.mult)
                half = ROPE // 2
                qr_ = qm_h[b][:, :, NOPE:QK]
                kr_ = proj[b][:, O_KR:O_KR + ROPE]
                link(V.tensor_tensor(qr_, qr_, rope_gain[:, 0, :].unsqueeze(1).to_broadcast([P, NH, ROPE]), ALU.mult),
                     V.tensor_tensor(kr_, kr_, rope_gain[:, 1, :], ALU.mult))
                tab = [rope_tab[:, f, b, :] for f in range(2)]
                tmp = [rope_tmp[i].rearrange("p (h c) -> p h c", h=NH) for i in range(4)]
                ops = []
                for i, (part, f) in enumerate(((0, 0), (1, 1), (0, 1), (1, 0))):
                    ops.append(V.tensor_tensor(tmp[i], qr_[:, :, part * half:part * half + half], tab[f].unsqueeze(1).to_broadcast([P, NH, half]), ALU.mult))
                link(*ops)
                if b:
                    dve.wait_ge(headT_mm, GROUPS_OF_TILE)
                qp = qpad.rearrange("p (a r d) -> p a r d", r=2, d=128)
                ops = []
                for r in range(2):
                    t4 = [t.rearrange("p (a r) c -> p a r c", r=2)[:, :, r, :] for t in tmp]
                    ops.append(V.tensor_tensor(qp[:, :, r, r * ROPE:r * ROPE + half], t4[0], t4[1], ALU.subtract))
                    ops.append(V.tensor_tensor(qp[:, :, r, r * ROPE + half:r * ROPE + ROPE], t4[2], t4[3], ALU.add))
                link(*ops)
                kt = rope_tmp[0]
                ops = []
                for i, (part, f) in enumerate(((0, 0), (1, 1), (0, 1), (1, 0))):
                    ops.append(V.tensor_tensor(kt[:, i * half:i * half + half], kr_[:, part * half:part * half + half], tab[f], ALU.mult))
                link(*ops)
                rot = rope_tmp[4]
                link(V.tensor_tensor(rot[:, 0:half], kt[:, 0:half], kt[:, half:2 * half], ALU.subtract),
                     V.tensor_tensor(rot[:, half:ROPE], kt[:, 2 * half:3 * half], kt[:, 3 * half:4 * half], ALU.add))
                V.tensor_tensor(krot.rearrange("p (h d) -> p h d", h=NH), rot.unsqueeze(1).to_broadcast([P, NH, ROPE]), per_head(1, ROPE), ALU.mult).then_inc(tok_ready, 1)

            for c in range(TT * IH // 2):
                b, pr = c // (IH // 2), c % (IH // 2)
                S = P * (b + 1)
                acc = work[b][:, 0:S]
                dve.wait_ge(relu_done, c + 1)
                for r in range(2):
                    h = 2 * pr + r
                    w = proj[b][:, O_WI + h:O_WI + h + 1]
                    dot = relu_buf[c % 2][:, r * S:r * S + S]
                    if h == 0:
                        link(V.tensor_scalar(acc, dot, w, None, ALU.mult))
                    else:
                        link(V.scalar_tensor_tensor(acc, dot, w, acc, ALU.mult, ALU.add))
                V.tensor_copy(top8, relu_buf[c % 2][:, 0:8]).then_inc(acc_done, 1)
            dve.wait_ge(acc_done, TT * IH // 2)
            dve.wait_ge(bias_in, 32)
            for b in range(TT):
                S = P * (b + 1)
                left = work[b][:, 0:S]
                link(V.tensor_tensor(left, left, chunk_mask[:, b, 0:S], ALU.add))
                for _ in range(N_SEL // 8):
                    link(V.max(top8, left))
                    link(V.match_replace(left, top8, left, REMOVED))
                link(V.tensor_scalar(left, left, REMOVED / 2, MASKED, ALU.is_gt, ALU.mult))
                link(V.tensor_tensor(bias[b][:, :, 0:S], bias[b][:, :, 0:S], left.unsqueeze(1).to_broadcast([P, NH, S]), ALU.add))

            def logits(j):
                g, pr, b = JOBS[j]
                S = P * (b + 1)
                dve.wait_ge(logit_mm, j + 1)
                if j >= 2:
                    dve.wait_ge(pT_mm, j - 1)
                ops = []
                for hh in range(2):
                    h = 2 * pr + hh
                    add = bias[b][:, h, 0:S] if g else chunk_mask[:, b, 0:S]
                    ops.append(V.scalar_tensor_tensor(logit[j % 2][:, hh * S:hh * S + S], ps[:, j % 2, hh * S:hh * S + S],
                                                      rs_h[:, b, 2 * g, h:h + 1], add, ALU.mult, ALU.add))
                link(*ops)
                V.tensor_reduce(j_nmax[:, 2 * j:2 * j + 2], logit[j % 2][:, 0:2 * S].rearrange("p (h s) -> p h s", h=2), AX, ALU.max, negate=True).then_inc(logit_done, 1)

            def normalise(j):
                S = P * (JOBS[j][2] + 1)
                dve.wait_ge(exp_done, j + 1)
                link(V.reciprocal(j_rec[:, 2 * j:2 * j + 2], j_sum[:, 2 * j:2 * j + 2]))
                for hh in range(2):
                    part = logit[j % 2][:, hh * S:hh * S + S]
                    ins = V.tensor_scalar(part, part, j_rec[:, 2 * j + hh:2 * j + hh + 1], None, ALU.mult)
                ins.then_inc(prob_done, 1)

            def y_lo(j):
                g, pr, b = JOBS[j]
                k = g * NH + 2 * pr
                dve.wait_ge(yhi_done, j + 1)
                V.tensor_tensor(hT_lo[:, k:k + 2, b * P:b * P + P], ps[:, 4 + j % 2, 0:256].rearrange("p (h t) -> p h t", h=2),
                                hT_hi[:, k:k + 2, b * P:b * P + P].bitcast(F32), ALU.subtract).then_inc(ylo_done, 1)
            for step in range(len(JOBS) + 2):
                if step < len(JOBS):
                    logits(step)
                if 1 <= step <= len(JOBS):
                    normalise(step - 1)
                if step >= 2:
                    y_lo(step - 2)

            def residual(n):
                dve.wait_ge(piece_used, 2 * B_WO + 16 * n + 16)
                for b in range(TT):
                    cols = xs[b][:, n * 512:n * 512 + 512]
                    V.tensor_tensor(cols, ps[:, 2 * (n % 2) + b, :], cols, ALU.add).then_inc(x2_done, 1)
            for n in range(D // 512):
                for j in range(8):
                    split_lo(B_WO + 8 * n + j, j)
                    if j == 1 and n:
                        if n == 1:
                            dve.wait_ge(x_back, 16)
                        residual(n - 1)
            residual(D // 512 - 1)

            norm_scale(1)
            norm_lo(1, G_FFN)
            with dve.Fori(0, U_PQ // 4) as i:
                for j in range(4):
                    split_lo(i * 4 + (B_PQ + j), j)

            dve.wait_ge(score_done, 8)
            steps = 15
            with dve.Fori(0, TT * NH) as i:
                count = [0]

                def step(*ins):
                    ins[-1].then_inc(head_step, 1)
                    count[0] += 1
                    dve.wait_ge(head_step, i * steps + count[0])
                    V.memset(carrier, 0.0)

                def split(j):
                    split_lo(i * 8 + (B_U + j), j)
                halves = [h_score[:, f, :] for f in range(2)]
                split(0)
                step(V.tensor_copy(h_score, acts[:, ds(i * 256 + A_SCORE, 256)].rearrange("p (f n) -> p f n", f=2)))
                step(*[V.max(top_v[:, f, 0:8], halves[f]) for f in range(2)])
                split(1)
                step(*[V.max_index(top_iu[:, f, 0:8], top_v[:, f, 0:8], halves[f]) for f in range(2)],
                     *[V.match_replace(halves[f], top_v[:, f, 0:8], halves[f], REMOVED) for f in range(2)])
                step(*[V.max(top_v[:, f, 8:16], halves[f]) for f in range(2)])
                split(2)
                step(*[V.max_index(top_iu[:, f, 8:16], top_v[:, f, 8:16], halves[f]) for f in range(2)])
                step(V.tensor_copy(top_i, top_iu),
                     V.tensor_tensor(cand.rearrange("p (i j) -> p i j", i=TOPK), top_v[:, 0, :].unsqueeze(2).to_broadcast([P, TOPK, TOPK]),
                                     top_v[:, 1, :].unsqueeze(1).to_broadcast([P, TOPK, TOPK]), ALU.add))
                split(3)
                step(V.max(c_v[:, 0:8], cand))
                step(V.max_index(c_iu[:, 0:8], c_v[:, 0:8], cand), V.match_replace(cand, c_v[:, 0:8], cand, REMOVED))
                split(4)
                step(V.max(c_v[:, 8:16], cand))
                step(V.max_index(c_iu[:, 8:16], c_v[:, 8:16], cand))
                split(5)
                step(V.tensor_scalar(c_digit_u[:, 0, :], c_iu, 4, None, ALU.logical_shift_right),
                     V.tensor_scalar(c_digit_u[:, 1, :], c_iu, 15, None, ALU.bitwise_and))
                step(V.tensor_copy(c_digit, c_digit_u))
                split(6)
                step(V.tensor_tensor(pick, c_digit.unsqueeze(3).to_broadcast([P, 2, TOPK, TOPK]),
                                     iota[:, 0:TOPK].unsqueeze(1).unsqueeze(1).to_broadcast([P, 2, TOPK, TOPK]), ALU.is_equal))
                step(V.tensor_tensor(pick, pick, top_i.unsqueeze(2).to_broadcast([P, 2, TOPK, TOPK]), ALU.mult))
                split(7)
                for f in range(2):
                    V.tensor_reduce(acts[:, ds(i * TOPK + (A_SLOT + f * SEQ), TOPK)], pick[:, f], AX, ALU.add)
                V.tensor_scalar(acts[:, ds(i * TOPK + (A_SLOT + 2 * SEQ), TOPK)], c_v, c_v[:, 0:1], None, ALU.subtract).then_inc(slot_ready, 1)
                step(V.tensor_copy(top8, c_v[:, 0:8]))
                assert count[0] == steps

            dve.wait_ge(cexp_done, 1)
            gates = slot[:, 2, :].rearrange("p (h j) -> p h j", j=TOPK)
            link(V.tensor_reduce(gate_sum[:, 0, :], gates, AX, ALU.add))
            link(V.reciprocal(gate_sum[:, 1, :], gate_sum[:, 0, :]))
            V.tensor_tensor(gates, gates, gate_sum[:, 1, :].unsqueeze(2).to_broadcast([P, TT * NH, TOPK]), ALU.mult).then_inc(slot_done, 1)
            for b in range(TT):
                dve.wait_ge(slotT_mm, b + 1)
                V.tensor_copy(slotT[:, :, b * P:b * P + P], ps[:, 6 + b, 0:384].rearrange("p (f t) -> p f t", f=3)).then_inc(slotT_done, 1)
            dve.wait_ge(slotT_done, TT)
            dve.wait_ge(ones_set, 3)

            slotT_flat = slotT[:, :, :].rearrange("p f t -> p (f t)")

            def hots(g):
                for k in range(4):
                    if not (isinstance(g, int) and g == 0):
                        dve.wait_ge(gate_mm, g * 4 + (k - 3))
                    V.tensor_scalar(hot1[k], iota[:, :], slotT_flat[:, ds(g * 4 + (k + SEQ), 1)], None, ALU.is_equal)
                    V.tensor_scalar(hot0[k], iota[:, :], slotT_flat[:, ds(g * 4 + k, 1)], slotT_flat[:, ds(g * 4 + (k + 2 * SEQ), 1)],
                                    ALU.is_equal, ALU.mult).then_inc(hot_done, 1)

            def gate(g, par):
                dve.wait_ge(gate_mm, g * 4 + 4)
                a = acts_e[:, :, ds(g * 4, 4)].rearrange("p e t -> p t e")
                V.tensor_tensor(a, a, ps[:, 2 + par, :].rearrange("p (t e) -> p t e", t=4), ALU.mult).then_inc(gated, 1)

            def apply(c, par, g, groups):
                dve.wait_ge(gelu_done, c + 1)
                dve.wait_ge(gated, groups)
                col = acts[:, ds(c * SEQ, SEQ)]
                V.tensor_tensor(col, col, gelu_buf[par], ALU.mult).then_inc(applied, 1)

            def second_half(i, first):
                g = i * 2 - NKEY // 2
                split_lo(i * 4 + B_U, 0)
                hots(g)
                split_lo(i * 4 + (B_U + 1), 1)
                if not first:
                    dve.wait_ge(applied, g - 1)
                    gate(g - 1, 1)
                    apply(i * 2 - 1, 1, g, g)
                split_lo(i * 4 + (B_U + 2), 2)
                hots(g + 1)
                split_lo(i * 4 + (B_U + 3), 3)
                if not first:
                    dve.wait_ge(applied, g)
                gate(g, 0)
                apply(i * 2, 0, g, g + 1)
            dve.wait_ge(gelu_done, NKEY // 2)
            second_half(NKEY // 4, True)
            with dve.Fori(NKEY // 4 + 1, NKEY // 2) as i:
                second_half(i, False)
            dve.wait_ge(applied, NKEY // 2 - 1)
            gate(SEQ // 4 - 1, 1)
            apply(NKEY - 1, 1, None, SEQ // 4)
            dve.wait_ge(gated, SEQ // 4)
            dve.wait_ge(applied, NKEY // 2)

            def expert_pair(i):
                for j in range(4):
                    if j % 2 == 0:
                        dve.wait_ge(ehi_done, i * 2 + (j // 2 + 1))
                        V.tensor_tensor(elo[j // 2][:, :], acts[:, ds(i * (2 * SEQ) + (j // 2) * SEQ, SEQ)], ehi[j // 2][:, :].bitcast(F32),
                                        ALU.subtract).then_inc(elo_done, 1)
                    split_lo(i * 4 + (B_V + j), j)
            with dve.Fori(0, NKEY // 2) as i:
                expert_pair(i)
            dve.wait_ge(x2_back, 16)
            dve.wait_ge(piece_used, 2 * B_END)
            for g in range(8):
                b, n = g // 4, g % 4
                V.tensor_tensor(xn[b][:, n * 512:n * 512 + 512], ps[:, g, :], xs[b][:, n * 512:n * 512 + 512], ALU.add).then_inc(out_ready, 1)

        @block.tensor
        def _(pe):
            mm = nc.tensor.matmul

            pe.wait_ge(hot_in, 32)
            mm(ps[0:8, 7, :], acts[0:32, A_BIAS + 512:A_BIAS + 520], acts[0:32, A_BIAS:A_BIAS + 512], start=True, stop=True).then_inc(vec_mm, 1)

            def norm_transpose(nth):
                pe.wait_ge(xn_done, TT * nth + TT)
                for k in range(KD):
                    if k == 7 and nth == 0:
                        pe.wait_ge(vec_ready, 1)
                    if k >= 8:
                        pe.wait_ge(hTlo_done, nth * KD + k - 7)
                    for b in range(TT):
                        ins = nc.tensor.transpose(ps[:, k % 8, b * P:b * P + P], xn[b][:, k * P:k * P + P], ident[:, :])
                    ins.then_inc(xT_mm, 1)

            pe.wait_ge(const_in, 16)
            norm_transpose(0)

            def tall_block(base, n, par, w):
                for k in range(KD):
                    pe.wait_ge(lo_done, n * 16 + (2 * base + k + 1))
                    for b in range(TT):
                        out = ps[:, 2 * par + b, 0:w]
                        t = slice(b * P, b * P + P)
                        mm(out, hT_hi[:, k, t], whi[k % NPART][:, 0:w], start=k == 0, stop=False)
                        mm(out, hT_hi[:, k, t], wlo[k % NPART][:, 0:w], start=False, stop=False)
                        ins = mm(out, hT_lo[:, k, t], whi[k % NPART][:, 0:w], start=False, stop=k == KD - 1)
                    ins.then_inc(piece_used, 1)

            pe.wait_ge(hTlo_done, KD)
            tall_block(0, 0, 0, 512)
            tall_block(0, 1, 1, 512)
            with pe.Fori(1, N_IN // 2 - 1) as i:
                for par in range(2):
                    pe.wait_ge(proj_done, i * 2 + (par - 1))
                    tall_block(0, i * 2 + par, par, 512)
            for n in (N_IN - 2, N_IN - 1):
                pe.wait_ge(proj_done, n - 1)
                tall_block(0, n, n % 2, width(n))

            pe.wait_ge(cn_done, 2 * TT)
            for k in range(6):
                off = O_CQ + P * k if k < 4 else O_CKV + P * (k - 4)
                for b in range(TT):
                    ins = nc.tensor.transpose(ps[:, k, b * P:b * P + P], proj[b][:, off:off + P], ident[:, :])
                ins.then_inc(cT_mm, 1)
            pe.wait_ge(cT_done, 6)
            pe.wait_ge(wu_in, 32)
            for g in range(14):
                b, n = g // 7, g % 7
                if g >= 8:
                    pe.wait_ge(up_done, g - 7)
                src, w, ks = (cqT, w_uq[:, :, n * 512:n * 512 + 512], 4) if n < 3 else (ckvT, w_ukv[:, :, (n - 3) * 512:(n - 3) * 512 + 512], 2)
                for k in range(ks):
                    ins = mm(ps[:, g % 8, :], src[:, k, b * P:b * P + P], w[:, k, :], start=k == 0, stop=k == ks - 1)
                ins.then_inc(up_mm, 1)

            pe.wait_ge(h_root, 4)
            for g, (srcs, dst, gain, need) in enumerate(GROUPS):
                pe.wait_ge(tok_ready, need)
                if g >= 8:
                    pe.wait_ge(headT_done, g - 7)
                for i, src in enumerate(srcs):
                    ins = nc.tensor.transpose(ps[:, g % 8, i * P:i * P + P], src, ident[:, :])
                ins.then_inc(headT_mm, 1)

            pe.wait_ge(headT_done, len(GROUPS))
            for c in range(TT * IH // 2):
                b, pr = c // (IH // 2), c % (IH // 2)
                S = P * (b + 1)
                if c >= 2:
                    pe.wait_ge(relu_done, c - 1)
                for r in range(2):
                    ins = mm(ps[:, 6 + c % 2, r * S:r * S + S], qiT[:, pr, b * P:b * P + P], kiT[:, r, 0:S], start=True, stop=True)
                ins.then_inc(dot_mm, 1)

            def products(j):
                g, pr, b = JOBS[j]
                S = P * (b + 1)
                t = slice(b * P, b * P + P)
                if j >= 2:
                    pe.wait_ge(logit_done, j - 1)
                for hh in range(2):
                    h = 2 * pr + hh
                    out = ps[:, j % 2, hh * S:hh * S + S]
                    if g == 0:
                        mm(out, qTn[:, h, t], kTn[:, h, 0:S], start=True, stop=False)
                        ins = mm(out, qTr[:, h, t], kTr[:, pr, 0:S], start=False, stop=True)
                    else:
                        ins = mm(out, qdT[:, h, t], kdT[:, h, 0:S], start=True, stop=True)
                ins.then_inc(logit_mm, 1)

            def prob_transpose(j):
                b = JOBS[j][2]
                pe.wait_ge(prob_done, j + 1)
                if j >= 2:
                    pe.wait_ge(pT_done, j - 1)
                for i in range(2 * (b + 1)):
                    ins = nc.tensor.transpose(ps[:, 2 + j % 2, i * P:i * P + P], logit[j % 2][:, i * P:i * P + P], ident[:, :])
                ins.then_inc(pT_mm, 1)

            def values(j):
                g, pr, b = JOBS[j]
                pe.wait_ge(pT_done, j + 1)
                if j >= 2:
                    pe.wait_ge(ylo_done, j - 1)
                for hh in range(2):
                    h = 2 * pr + hh
                    for s in range(b + 1):
                        v = proj[s][:, O_VD + h * HD:O_VD + h * HD + HD] if g else kv_h[s][:, h, NOPE:NOPE + HD]
                        i = hh * (b + 1) + s
                        ins = mm(ps[:, 4 + j % 2, hh * P:hh * P + P], v, probT[j % 2][:, i * P:i * P + P], start=s == 0, stop=s == b)
                ins.then_inc(y_mm, 1)
            for step in range(len(JOBS) + 2):
                if step < len(JOBS):
                    products(step)
                if 1 <= step <= len(JOBS):
                    prob_transpose(step - 1)
                if step >= 2:
                    values(step - 2)

            pe.wait_ge(ylo_done, len(JOBS))
            tall_block(B_WO, 0, 0, 512)
            tall_block(B_WO, 1, 1, 512)
            for n in (2, 3):
                pe.wait_ge(x2_done, TT * (n - 1))
                tall_block(B_WO, n, n % 2, 512)
            pe.wait_ge(x2_done, 8)
            norm_transpose(1)

            def wide_piece(i, base, j, c):
                pe.wait_ge(lo_done, i * 8 + (2 * base + j + 1))
                for kk in range(4):
                    k = 4 * (j % 4) + kk
                    w = slice(kk * P, kk * P + P)
                    out = ps[:, c, 0:SEQ]
                    mm(out, whi[j % NPART][:, w], hT_hi[:, k, :], start=k == 0, stop=False)
                    mm(out, whi[j % NPART][:, w], hT_lo[:, k, :], start=False, stop=False)
                    ins = mm(out, wlo[j % NPART][:, w], hT_hi[:, k, :], start=False, stop=k == KD - 1)
                ins.then_inc(piece_used, 1)

            def wide_pair(i, base, out_done):
                for c in range(2):
                    if not (isinstance(i, int) and i == 0):
                        pe.wait_ge(out_done, i * 2 + (c - 1))
                    for j in range(4):
                        wide_piece(i, base, 4 * c + j, c)

            pe.wait_ge(hTlo_done, 2 * KD)
            wide_pair(0, B_PQ, qr_done)
            with pe.Fori(1, U_PQ // 4) as i:
                wide_pair(i, B_PQ, qr_done)
            pe.wait_ge(qr_done, 16)
            pe.wait_ge(subk_in, 16)
            for g in range(8):
                b, q = g // 4, g % 4
                if g >= 4:
                    pe.wait_ge(score_done, g - 3)
                for i in range(4):
                    c = 4 * q + i
                    ins = mm(ps[:, 2 + g % 4, i * P:i * P + P], qr[:, c, b * P:b * P + P], subk[:, c, :], start=True, stop=True)
                ins.then_inc(score_mm, 1)
            wide_pair(0, B_U, gelu_done)
            with pe.Fori(1, NKEY // 4) as i:
                wide_pair(i, B_U, gelu_done)
            pe.wait_ge(slot_done, 1)
            for b in range(TT):
                for f in range(3):
                    ins = nc.tensor.transpose(ps[:, 6 + b, f * P:f * P + P], slot[:, f, b * P:b * P + P], ident[:, :])
                ins.then_inc(slotT_mm, 1)

            def gate_group(g, q, first):
                if not first:
                    pe.wait_ge(gated, g - 1)
                for k in range(4):
                    pe.wait_ge(hot_done, g * 4 + (k + 1))
                    mm(ps[:, 2 + q, k * P:k * P + P], hot1[k], hot0[k], start=True, stop=True).then_inc(gate_mm, 1)

            def second_half(i, first):
                for c in range(2):
                    pe.wait_ge(gelu_done, i * 2 + (c - 1))
                    for j in range(4):
                        wide_piece(i, B_U, 4 * c + j, c)
                        if j == 2:
                            gate_group(i * 2 + (c - NKEY // 2), c, first)
            second_half(NKEY // 4, True)
            with pe.Fori(NKEY // 4 + 1, NKEY // 2) as i:
                second_half(i, False)

            pe.wait_ge(gated, SEQ // 4)

            def expert_pair(i, first, last):
                for c in range(2):
                    pe.wait_ge(elo_done, i * 2 + (c + 1))
                    for q in range(4):
                        pe.wait_ge(lo_done, i * 8 + (2 * B_V + 4 * c + q + 1))
                        start, stop = first and c == 0, last and c == 1
                        for b in range(TT):
                            t = slice(b * P, b * P + P)
                            out = ps[:, 4 * b + q, :]
                            mm(out, ehi[c][:, t], whi[q][:, :], start=start, stop=False)
                            mm(out, ehi[c][:, t], wlo[q][:, :], start=False, stop=False)
                            ins = mm(out, elo[c][:, t], whi[q][:, :], start=False, stop=stop)
                        ins.then_inc(piece_used, 1)
            expert_pair(0, True, False)
            with pe.Fori(1, NKEY // 2 - 1) as i:
                expert_pair(i, False, False)
            expert_pair(NKEY // 2 - 1, False, True)

    return nc


def t5_bucket_of_distance(rel):
    n = np.abs(rel)
    nf = np.maximum(n, 1).astype(np.float32)
    large = 8 + (np.log(nf / np.float32(8)) / np.float32(math.log(16)) * np.float32(8)).astype(np.int32)
    return np.where(rel > 0, 16, 0) + np.where(n < 8, n, np.minimum(large, 15))


def shape_constants(seq):
    half, chunk, tiles = 32, 64, seq // 128
    pos = np.arange(seq)
    freqs = np.float32(10000.0) ** (np.float32(-2.0) * np.arange(half, dtype=np.float32) / np.float32(2 * half))
    ang = pos.astype(np.float32)[:, None] * freqs[None, :]
    rope = np.stack([np.cos(ang), np.sin(ang)]).reshape(2, tiles, 128, half).transpose(2, 0, 1, 3).reshape(128, -1)
    mask = np.where(pos[None, :] // chunk <= pos[:, None] // chunk, 0.0, -1.0e30)
    mask = mask.reshape(tiles, 128, seq).transpose(1, 0, 2).reshape(128, -1)
    distance = np.arange(512) - (seq - 1)
    hot = np.arange(32)[:, None] == t5_bucket_of_distance(distance)[None, :]
    made = {
        "ident": np.eye(128), "iota": np.tile(np.arange(128), (128, 1)), "eps": np.full((128, 1), 1e-6),
        "rope_tab": rope, "chunk_mask": mask, "bucket_hot": hot,
    }
    return {n: np.ascontiguousarray(a, dtype=np.float32) for n, a in made.items()}


def kernel(**inputs):
    import concourse.bacc as _bacc
    from concourse import mybir as _mybir
    from concourse.bass_utils import run_bass_kernel_spmd as _run

    a = {n: np.asarray(v) for n, v in inputs.items()}
    seq, d = a["x"].shape[1:]
    columns = lambda g: g.reshape(-1, 128).T
    sent = {
        "x": a["x"][0], "w_in": a["w_in"][0], "w_uq": a["w_uq"][0], "w_ukv": a["w_ukv"][0], "w_o": a["w_o"][0],
        "rel_bias": a["rel_bias"], "v_tab": a["v_tab"][0],
        "gains": np.concatenate([columns(a["g_attn"]), columns(a["g_ffn"]), columns(a["g_cq"]), columns(a["g_ckv"]),
                                 columns(a["g_mla_q"][:, 0:128]), columns(a["g_mla_k"][:, 0:128]), columns(a["g_dsa_q"]), columns(a["g_dsa_k"])], axis=1),
        "rope_gain": np.concatenate([a["g_mla_q"][:, 128:], a["g_mla_k"][:, 128:]], axis=1),
        "w_pq": a["w_pq"][0].reshape(2, 8, 128, 16, 128).transpose(3, 0, 2, 1, 4).reshape(-1, 1024),
        "u_tab": a["u_tab"][0].reshape(128, 128, 2, 8, 128).transpose(0, 2, 4, 3, 1).reshape(-1, 1024),
        "sub_keys": a["sub_keys"][0].reshape(16, 128, 128).transpose(2, 0, 1),
    }
    arrays = {f"in_{n}": np.ascontiguousarray(v) for n, v in {**sent, **shape_constants(seq)}.items()}
    nc = _bacc.Bacc("TRN2", target_bir_lowering=False, num_devices=1)
    f32 = _mybir.dt.float32
    io = {n[3:]: nc.dram_tensor(n, v.shape, _mybir.dt.from_np(v.dtype), kind="ExternalInput").ap() for n, v in arrays.items()}
    io["out"] = nc.dram_tensor("out_0", (seq, d), f32, kind="ExternalOutput").ap()
    io["x2_scratch"] = nc.dram_tensor("x2_scratch", (seq, d), f32, kind="Internal").ap()
    io["bias_scratch"] = nc.dram_tensor("bias_scratch", (8, 128, 512), f32, kind="Internal").ap()
    build_block(nc, io)
    r = _run(nc, [arrays], core_ids=[0])
    return r.results[0]["out_0"].reshape(1, seq, d)
```

```python
import math
from contextlib import ExitStack

import concourse.bass as bass
import numpy as np
from concourse import mybir


def build_block(nc, io):
    F32 = mybir.dt.float32
    F32R = mybir.dt.float32r
    U32 = mybir.dt.uint32
    ALU = mybir.AluOpType
    ACT = mybir.ActivationFunctionType
    AX = mybir.AxisListType.X
    ds = bass.ds

    P = 128
    SEQ, D = io["x"].shape
    TT = SEQ // P
    KD = D // P
    IN_W = io["w_in"].shape[1]
    QL, CKV, ROPE = 512, 256, 64
    NH, NOPE, HD = 8, 128, 128
    QK = NOPE + ROPE
    IH, ID = 16, 64
    N_SEL = SEQ // 4
    TOPK, NKEY = 16, 128
    EPS = 1e-6
    MASKED, REMOVED = -1.0e30, -3.0e38
    O_CQ, O_CKV, O_KR = 0, QL, QL + CKV
    O_QD = O_KR + ROPE
    O_KD = O_QD + NH * HD
    O_VD = O_KD + NH * HD
    O_QI = O_VD + NH * HD
    O_KI = O_QI + IH * ID
    O_WI = O_KI + ID
    assert O_WI + IH == IN_W

    UNIT = 1024
    PIECE = UNIT // 2
    NRAW, NPART = 4, 4
    N_IN = -(-IN_W // 512)
    LAST_W = IN_W - 512 * (N_IN - 1)
    U_IN, U_WO, U_PQ = 8 * N_IN, 8 * (D // 512), 2 * 16
    NX = 4
    XW = D // NX
    B_IN = 0
    B_WO = B_IN + U_IN
    B_PQ = B_WO + U_WO
    B_U = B_PQ + U_PQ
    B_V = B_U + 2 * NKEY
    B_END = B_V + 2 * NKEY

    with ExitStack() as ctx:
        def sb(name, shape, dt=F32):
            return ctx.enter_context(nc.sbuf_tensor(name, shape, dt))

        def sem(name):
            return ctx.enter_context(nc.semaphore(name))

        acts = sb("acts", [P, NKEY * SEQ])
        hT_hi = sb("hT_hi", [P, KD, SEQ], F32R)
        hT_lo = sb("hT_lo", [P, KD, SEQ], F32R)
        raw = [sb(f"raw{i}", [P, UNIT]) for i in range(NRAW)]
        whi = [sb(f"w_hi{i}", [P, PIECE], F32R) for i in range(NPART)]
        wlo = [sb(f"w_lo{i}", [P, PIECE], F32R) for i in range(NPART)]
        ehi = [sb(f"e_hi{i}", [P, SEQ], F32R) for i in range(2)]
        elo = [sb(f"e_lo{i}", [P, SEQ], F32R) for i in range(2)]
        ident = sb("ident", [P, P])
        iota = sb("iota", [P, P])
        eps = sb("eps", [P, 1])
        gains = sb("gains", [P, 2 * KD + 10])
        slotT = sb("slotT", [P, 3, SEQ])
        early = sb("early", [P, 1536])
        stat = sb("stat", [P, 288])
        junk = sb("junk", [P, 192], mybir.dt.bfloat16)
        ps = ctx.enter_context(nc.psum_tensor("ps", [P, 8, 512], F32))

        G_ATTN, G_FFN, G_CQ, G_CKV, G_MQ, G_MK, G_DQ, G_DK = 0, KD, 2 * KD, 2 * KD + 4, 2 * KD + 6, 2 * KD + 7, 2 * KD + 8, 2 * KD + 9

        ckvT = early[:, 0:512].rearrange("p (k t) -> p k t", k=2)
        chunk_mask = early[:, 512:1024].rearrange("p (b s) -> p b s", b=TT)
        kpad = early[:, 1024:1280].rearrange("p (r d) -> p r d", r=2)
        rope_tab = early[:, 1280:1408].rearrange("p (f b c) -> p f b c", f=2, b=TT)
        rope_gain = early[:, 1408:1536].rearrange("p (f c) -> p f c", f=2)
        diag = [early[:, P * b:P * b + P] for b in range(TT)]
        krot = early[:, 0:512]
        hot1 = [early[:, 128 * i:128 * i + 128] for i in range(4)]
        hot0 = [early[:, 512 + 128 * i:512 + 128 * i + 128] for i in range(4)]
        gelu_buf = [early[:, 1024 + SEQ * i:1024 + SEQ * i + SEQ] for i in range(2)]

        def region(at, n):
            return acts[:, at:at + n]

        proj = [region(b * IN_W, IN_W) for b in range(TT)]
        A_WU = TT * IN_W
        w_uq = region(A_WU, 6144).rearrange("p (k n) -> p k n", k=4)
        w_ukv = region(A_WU + 6144, 4096).rearrange("p (k n) -> p k n", k=2)
        head_view = lambda at, n=8: region(at, n * SEQ).rearrange("p (h t) -> p h t", h=n)
        qTn, qTr, kTn = head_view(A_WU), head_view(A_WU + 2048), head_view(A_WU + 4096)
        kTr = head_view(A_WU + 6144, 4)
        qiT = head_view(A_WU + 7168)
        kiT = head_view(A_WU + 9216, 2)
        A_KV = A_WU + 10240
        kv = [region(A_KV + 2048 * b, 2048) for b in range(TT)]
        A_BIAS = A_KV + 4096
        xT = region(A_KV, KD * SEQ).rearrange("p (k t) -> p k t", k=KD)
        bias = [region(A_BIAS + 2048 * b, 2048).rearrange("p (h s) -> p h s", h=NH) for b in range(TT)]
        A_QM = A_BIAS + 4096
        qm = [region(A_QM + 1536 * b, 1536) for b in range(TT)]
        A_TAIL = A_QM + 3072
        cqT = region(A_TAIL, 1024).rearrange("p (k t) -> p k t", k=4)
        qpad = region(A_TAIL, 1024)
        qdT, kdT = head_view(A_QM), head_view(A_QM + 2048)
        assert A_TAIL + 1024 <= NKEY * SEQ
        rope_tmp = [proj[0][:, 256 * i:256 * i + 256] for i in range(3)] + [proj[1][:, 0:256], proj[1][:, 256:320]]
        relu_buf = [proj[i][:, 0:512] for i in range(2)]
        work = [region(A_WU + 9728 + 256 * b, 256) for b in range(TT)]
        y_first = qiT
        logit = [proj[0][:, O_QI + 512 * i:O_QI + 512 * i + 512] for i in range(2)]
        probT = [proj[1][:, O_QI + 512 * i:O_QI + 512 * i + 512] for i in range(2)]
        A_VEC = A_BIAS + 1024
        xs = [region(D * b, D) for b in range(TT)]
        xn = [region(TT * D + D * b, D) for b in range(TT)]
        A_X2 = A_WU
        x2 = [region(A_X2 + D * b, D) for b in range(TT)]
        x2n = [region(D * b, D) for b in range(TT)]
        A_QR = TT * D
        qr = region(A_QR, 16 * SEQ).rearrange("p (c t) -> p c t", c=16)
        A_SUBK = A_X2 + TT * D
        subk = region(A_SUBK, 16 * NKEY).rearrange("p (c n) -> p c n", c=16)
        A_SCORE = NKEY * SEQ - TT * 2048
        A_TK = A_SCORE - 2560
        score = [region(A_SCORE + 2048 * b, 2048).rearrange("p (c n) -> p c n", c=16) for b in range(TT)]
        A_SLOT = A_TK
        slot = region(A_SLOT, 3 * SEQ).rearrange("p (f s) -> p f s", f=3)
        h_score = region(A_TK + 768, 256).rearrange("p (f n) -> p f n", f=2)
        cand = region(A_TK + 1024, 256)
        pick = region(A_TK + 1280, 512).rearrange("p (f k j) -> p f k j", f=2, k=TOPK)
        pair16 = lambda at: region(A_TK + 1792 + at, 32).rearrange("p (f j) -> p f j", f=2)
        top_v, top_iu, top_i, c_digit_u, c_digit = pair16(0), pair16(32).bitcast(U32), pair16(64), pair16(96).bitcast(U32), pair16(128)
        c_v, c_iu = region(A_TK + 1952, 16), region(A_TK + 1968, 16).bitcast(U32)
        gate_sum = region(A_TK + 1984, 32).rearrange("p (f j) -> p f j", f=2)
        acts_e = acts[:, :].rearrange("p (e t) -> p e t", t=SEQ)

        ss_x, rs_x = stat[:, 0:2], stat[:, 2:4]
        ss_c, rs_c = stat[:, 4:8], stat[:, 8:12]
        ss_kr = stat[:, 12:14]
        ss_h = stat[:, 16:80].rearrange("p (b k h) -> p b k h", b=TT, k=4)
        rs_h = stat[:, 80:144].rearrange("p (b k h) -> p b k h", b=TT, k=4)
        j_max, j_nmax = stat[:, 144:176], stat[:, 176:208]
        j_sum, j_rec = stat[:, 208:240], stat[:, 240:272]
        top8 = stat[:, 272:280]
        ss_part = stat[:, 272:280].rearrange("p (b n) -> p b n", b=TT)
        carrier, table_warm = stat[:, 280:281], stat[:, 281:282]

        raw_ready = [sem(f"raw_ready{i}") for i in range(NRAW)]
        hi_done, lo_done, piece_used = sem("hi_done"), sem("lo_done"), sem("piece_used")
        xT_in = [sem(f"xT_in{i}") for i in range(KD // 2)]
        x_in = [sem(f"x_in{i}") for i in range(NX)]
        const_in, gain_in, mask_in, wu_in = sem("const_in"), sem("gain_in"), sem("mask_in"), sem("wu_in")
        hot_in, vec_mm, vec_ready, vec_out, bias_in = sem("hot_in"), sem("vec_mm"), sem("vec_ready"), sem("vec_out"), sem("bias_in")
        x_back, subk_in, x2_done, x2_stored, x2_back = sem("x_back"), sem("subk_in"), sem("x2_done"), sem("x2_stored"), sem("x2_back")
        x_sq, x_sum, x_root, rs_ready, diag_done = sem("x_sq"), sem("x_sum"), sem("x_root"), sem("rs_ready"), sem("diag_done")
        xT_mm, hThi_done, hTlo_done = sem("xT_mm"), sem("hThi_done"), sem("hTlo_done")
        proj_done, c_root, cn_done = sem("proj_done"), sem("c_root"), sem("cn_done")
        side_mm, side_done = sem("side_mm"), sem("side_done")
        sq_done, ss_done, h_root, tok_ready, acc_done = sem("sq_done"), sem("ss_done"), sem("h_root"), sem("tok_ready"), sem("acc_done")
        first_hi, first_lo = sem("first_hi"), sem("first_lo")
        logit_mm, logit_done, exp_done, prob_done = sem("logit_mm"), sem("logit_done"), sem("exp_done"), sem("prob_done")
        pT_mm, pT_done, y_mm, yhi_done, ylo_done = sem("pT_mm"), sem("pT_done"), sem("y_mm"), sem("yhi_done"), sem("ylo_done")
        qr_done, score_mm, score_done = sem("qr_done"), sem("score_mm"), sem("score_done")
        head_step, slot_ready, cexp_done, slot_done = sem("head_step"), sem("slot_ready"), sem("cexp_done"), sem("slot_done")
        slotT_mm, slotT_done, ones_set, applied = sem("slotT_mm"), sem("slotT_done"), sem("ones_set"), sem("applied")
        gelu_done, hot_done, gate_mm, gated = sem("gelu_done"), sem("hot_done"), sem("gate_mm"), sem("gated")
        ehi_done, elo_done, out_ready, out_sent = sem("ehi_done"), sem("elo_done"), sem("out_ready"), sem("out_sent")
        dve_chain, act_chain = sem("dve_chain"), sem("act_chain")

        JOBS = [(g, pr, b) for g in range(2) for pr in range(NH // 2) for b in range(TT)]
        kv_h = [kv[b].rearrange("p (h d) -> p h d", h=NH) for b in range(TT)]
        qm_h = [qm[b].rearrange("p (h d) -> p h d", h=NH) for b in range(TT)]

        def head_blocks(src, off, g):
            return [src[:, off + 128 * (4 * g + i):off + 128 * (4 * g + i) + 128] for i in range(4)]

        def nope_blocks(src, g):
            return [src[:, 4 * g + i, 0:NOPE] for i in range(4)]

        W_IN_ORDER = [0, 1, 7, 8, 9, 2, 3, 4, 5, 6]
        SLOTS = 8 * (N_IN - 2) + 16
        LATENT_T = {2: (0, 1, 2, 3), 3: (4, 5)}
        UP_AT = 4
        SQ_FIRST = {8: (0, 0, 0), 9: (0, 0, 4), 12: (0, 1, 0), 13: (0, 1, 4), 15: (1, 0, 0), 16: (1, 0, 4), 19: (1, 1, 0), 20: (1, 1, 4)}
        ROOT_AT = (13, 20)
        ROPE_AT = (15, 22)
        QPAD_AT = (18, 23)
        KROT_AT = (19, 24)
        KPAD_AT = (26, 27)
        groups = []
        for b, slots in ((0, (18, 19, 20)), (1, (21, 24, 22))):
            t = slice(b * P, b * P + P)
            for g in range(2):
                groups.append((slots[0], nope_blocks(qm_h[b], g), qTn[:, 4 * g:4 * g + 4, t], G_MQ))
                groups.append((slots[1], head_blocks(qpad, 0, g), qTr[:, 4 * g:4 * g + 4, t], None))
                groups.append((slots[2], nope_blocks(kv_h[b], g), kTn[:, 4 * g:4 * g + 4, t], G_MK))
            groups.append((slots[1], head_blocks(krot, 0, 0), kTr[:, :, t], None))
        for b, slot_no in ((0, 26), (1, 28)):
            t = slice(b * P, b * P + P)
            for g in range(2):
                groups.append((slot_no, head_blocks(proj[b], O_QI, g), qiT[:, 4 * g:4 * g + 4, t], None))
            groups.append((slot_no, [kpad[:, r, :] for r in range(2)], kiT[:, :, t], None))
        for b in range(TT):
            t = slice(b * P, b * P + P)
            for g in range(2):
                groups.append((57, head_blocks(proj[b], O_QD, g), qdT[:, 4 * g:4 * g + 4, t], G_DQ))
                groups.append((61 + b, head_blocks(proj[b], O_KD, g), kdT[:, 4 * g:4 * g + 4, t], G_DK))
        groups.sort(key=lambda x: x[0])
        TOK_NEEDED = {19: 2, 20: 2, 22: 3, 24: 4, 26: 5, 28: 6, 61: 7, 62: 8}
        DOTS_AT, DOTS = 29, TT * IH // 2
        SELECT_AT = 38
        JOB_AT = [37 + 2 * j for j in range(8)] + [63 + j for j in range(8)]
        SQ_SECOND = {42 + i: [(i // 4, 2, 2 * (i % 4) + k) for k in range(2)] for i in range(8)}
        SQ_SECOND |= {50 + i: [(b, 3, i) for b in range(TT)] for i in range(5)}
        SQ_SECOND |= {57: [(b, 3, 5) for b in range(TT)] + [(0, 3, 6)], 58: [(1, 3, 6)] + [(b, 3, 7) for b in range(TT)]}
        SQ_NEEDED = {42: 7, 50: 8, 57: 9}
        ROOT2_AT = 59
        FIRST_AT = (58, 61, 62, 63)
        SIDE_UP = 6
        SIDE_T = SIDE_UP + 14
        N_EARLY = sum(g[0] < DOTS_AT for g in groups)
        SIDE_DOT = SIDE_T + N_EARLY
        SIDE_T2 = SIDE_DOT + DOTS
        SIDE_END = SIDE_T2 + len(groups) - N_EARLY

        def side_bank(x):
            return 4 + x % 4

        NT = 6

        def norm_bank(k):
            return 2 + k % NT

        def norm_chunk(nth, k):
            return ps[:, norm_bank(k), 0:SEQ] if nth else xT[:, k, :]

        block = ctx.enter_context(nc.Block())

        def width(n):
            return LAST_W if isinstance(n, int) and n == N_IN - 1 else 512

        @block.sync
        def _(sp):
            def load(u, j, src):
                if not (isinstance(u, int) and u < NRAW):
                    sp.wait_ge(lo_done, u * 2 - 2 * (NRAW - 1))
                dst = raw[j % NRAW][:, 0:src.free_size()]
                if len(src.shape) == 3:
                    dst = dst.rearrange("p (k n) -> p k n", k=src.shape[1])
                sp.dma_start(dst, src).then_inc(raw_ready[j % NRAW], 16)

            win = io["w_in"].rearrange("(k p) n -> p k n", p=P)
            for n in range(8):
                k = slice(2 * n, 2 * n + 2)
                sp.dma_start(xT[:, k, :], io["xT"][:, k, :]).then_inc(xT_in[n], 16)
                if n == 0:
                    sp.dma_start(gains[:, :], io["gains"]).then_inc(gain_in, 16)
                load(n, n, win[:, k, 0:512])
            sp.dma_start(ident[:, :], io["ident"]).then_inc(const_in, 16)
            sp.dma_start(eps[:, :], io["eps"]).then_inc(const_in, 16)
            for j in range(8):
                load(8 + j, j, win[:, 2 * j:2 * j + 2, 512:1024])
            with sp.Fori(7, N_IN - 1) as n:
                for j in range(8):
                    load(n * 8 + (j - 40), j, win[:, 2 * j:2 * j + 2, ds(n * 512, 512)])
            for j in range(8):
                load(32 + j, j, win[:, 2 * j:2 * j + 2, 512 * (N_IN - 1):IN_W])
            with sp.Fori(2, 7) as n:
                for j in range(8):
                    load(n * 8 + (24 + j), j, win[:, 2 * j:2 * j + 2, ds(n * 512, 512)])
            wo = io["w_o"].rearrange("(k p) n -> p k n", p=P)
            for group in range(2):
                with sp.Fori(0, D // 512) as n:
                    for j in range(4):
                        k = 8 * group + 2 * j
                        load(n * 4 + (B_WO + 16 * group + j), j, wo[:, k:k + 2, ds(n * 512, 512)])
            with sp.Fori(0, U_PQ // 4) as i:
                for j in range(4):
                    load(i * 4 + (B_PQ + j), j, io["w_pq"][ds(i * (4 * P) + j * P, P), :])
            with sp.Fori(0, 2 * NKEY // 4) as i:
                for j in range(4):
                    load(i * 4 + (B_U + j), j, io["u_tab"][ds(i * (4 * P) + j * P, P), :])
            with sp.Fori(0, 2 * NKEY // 4) as i:
                for j in range(4):
                    load(i * 4 + (B_V + j), j,
                         io["v_tab"][ds(i * (2 * P) + (j // 2) * P, P), (j % 2) * UNIT:(j % 2) * UNIT + UNIT])
            for g in range(8):
                n, b = g // TT, g % TT
                sp.wait_ge(out_ready, g + 1)
                sp.dma_start(io["out"][b * P:b * P + P, n * 512:n * 512 + 512], xn[b][:, n * 512:n * 512 + 512]).then_inc(out_sent, 16)
            sp.wait_ge(out_sent, 16 * 8)
            sp.wait_ge(x2_stored, 16)
            sp.wait_ge(vec_out, 16)

        @block.gpsimd
        def _(pool):
            pool.dma_start(acts[0:32, A_BIAS:A_BIAS + 512], io["bucket_hot"]).then_inc(hot_in, 16)
            pool.dma_start(acts[0:32, A_BIAS + 512:A_BIAS + 520], io["rel_bias"]).then_inc(hot_in, 16)
            pool.dma_start(iota[:, :], io["iota"]).then_inc(mask_in, 16)
            pool.dma_start(early[:, 1280:1408], io["rope_tab"]).then_inc(mask_in, 16)
            pool.dma_start(early[:, 512:1024], io["chunk_mask"]).then_inc(mask_in, 16)
            pool.dma_start(early[:, 1408:1536], io["rope_gain"].to_broadcast([P, 128])).then_inc(mask_in, 16)
            x_cols, x_rows = acts[:, 0:TT * D].rearrange("p (b d) -> p b d", b=TT), io["x"].rearrange("(b p) d -> p b d", p=P)
            for n in range(NX):
                pool.wait_ge(piece_used, 2 * n + 2)
                cols = slice(n * XW, n * XW + XW)
                pool.dma_start(x_cols[:, :, cols], x_rows[:, :, cols]).then_inc(x_in[n], 16)
            for i in range(6):
                pool.wait_ge(piece_used, 10 + 4 * i)
                dst, src, k = (w_uq, io["w_uq"], i) if i < 4 else (w_ukv, io["w_ukv"], i - 4)
                pool.dma_start(dst[:, k, :], src[k * P:k * P + P, :]).then_inc(wu_in, 16)
            pool.wait_ge(vec_ready, 1)
            pool.wait_ge(piece_used, 48)
            pool.dma_start(io["bias_scratch"], acts[0:8, A_VEC:A_VEC + 512].unsqueeze(1).to_broadcast([8, P, 512])).then_inc(vec_out, 16)
            pool.wait_ge(vec_out, 16)
            for b in range(TT):
                first = SEQ - 1 - b * P
                src = bass.AP(io["bias_scratch"].tensor, first, [[511, P], [512 * P, NH], [1, SEQ]])
                pool.dma_start(bias[b], src).then_inc(bias_in, 16)
            pool.wait_ge(logit_mm, 8)
            pool.dma_start(acts[:, A_X2:A_X2 + TT * D].rearrange("p (b d) -> p b d", b=TT), io["x"].rearrange("(b p) d -> p b d", p=P)).then_inc(x_back, 16)
            pool.wait_ge(ylo_done, 8)
            pool.dma_start(subk, io["sub_keys"]).then_inc(subk_in, 16)
            pool.wait_ge(x2_done, 16)
            pool.dma_start(io["x2_scratch"].rearrange("(b p) d -> p b d", p=P), acts[:, A_X2:A_X2 + TT * D].rearrange("p (b d) -> p b d", b=TT)).then_inc(x2_stored, 16)
            pool.wait_ge(x2_stored, 16)
            half = NKEY * SEQ // 2
            pool.memset(region(half, A_TK - half), 1.0).then_inc(ones_set, 1)
            pool.wait_ge(slot_ready, NH)
            pool.memset(region(A_SCORE, 2048), 1.0).then_inc(ones_set, 1)
            pool.wait_ge(slot_ready, 2 * NH)
            pool.memset(region(A_SCORE + 2048, 2048), 1.0).then_inc(ones_set, 1)
            pool.wait_ge(slotT_mm, TT)
            pool.memset(region(A_TK, 2560), 1.0).then_inc(ones_set, 1)
            pool.wait_ge(piece_used, 2 * B_V + 4 * (TT * D // SEQ))
            pool.dma_start(acts[:, 0:TT * D].rearrange("p (b d) -> p b d", b=TT), io["x2_scratch"].rearrange("(b p) d -> p b d", p=P)).then_inc(x2_back, 16)

        @block.scalar
        def _(act):
            links = [0]

            def link(*ins):
                for i in ins:
                    i.then_inc(act_chain, 1)
                links[0] += len(ins)
                act.wait_ge(act_chain, links[0])

            def split_hi(u, j, w=PIECE):
                act.wait_ge(raw_ready[j % NRAW], (u - j % NRAW) * (16 // NRAW) + 16)
                for half in range(2):
                    if not (isinstance(u, int) and 2 * u + half < NPART):
                        act.wait_ge(piece_used, u * 2 + (half + 1 - NPART))
                    nc.scalar.activation(whi[(2 * j + half) % NPART][:, 0:w], raw[j % NRAW][:, half * w:half * w + w], ACT.Copy).then_inc(hi_done, 1)

            def norm_square(nth, xs, junk_to, b, n):
                if nth:
                    act.wait_ge(x2_done, 2 * (4 + n) + b + 1)
                else:
                    act.wait_ge(x_in[n], 16)
                cols = slice(n * XW, n * XW + XW)
                nc.scalar.activation(junk_to[b][:, cols], xs[b][:, cols], ACT.Square, accum_out=ss_part[:, b, n:n + 1]).then_inc(x_sq, 1)

            def norm_root(nth):
                act.wait_ge(x_sum, nth + 1)
                nc.scalar.activation(rs_x, ss_x, ACT.Sqrt, bias=eps[:, :], scale=1.0 / D).then_inc(x_root, 1)

            def norm_hi(nth, gain, k):
                if nth:
                    act.wait_ge(xT_mm, k + 1)
                else:
                    act.wait_ge(xT_in[k // 2], 16)
                nc.scalar.activation(hT_hi[:, k, :], norm_chunk(nth, k), ACT.Copy,
                                     scale=gains[:, gain + k:gain + k + 1]).then_inc(hThi_done, 1)

            def proj_out(pos):
                n = W_IN_ORDER[pos]
                act.wait_ge(piece_used, 16 * pos + 16)
                for b in range(TT):
                    ins = nc.scalar.activation(proj[b][:, n * 512:n * 512 + width(n)], ps[:, 2 * (pos % 2) + b, 0:width(n)], ACT.Copy,
                                               scale=rs_x[:, b:b + 1])
                ins.then_inc(proj_done, 1)

            def side_out(x, dst, src, func=ACT.Copy, scale=1.0):
                act.wait_ge(side_mm, x + 1)
                nc.scalar.activation(dst, src, func, scale=scale).then_inc(side_done, 1)

            squares_so_far = [0]

            def sum_squares(b, kind, h):
                src = (qm_h[b][:, h, :], kv_h[b][:, h, 0:NOPE], proj[b][:, O_QD + h * HD:O_QD + h * HD + HD], proj[b][:, O_KD + h * HD:O_KD + h * HD + HD])[kind]
                if squares_so_far[0]:
                    act.wait_ge(sq_done, squares_so_far[0])
                squares_so_far[0] += 1
                nc.scalar.activation(junk[:, 0:src.free_size()], src, ACT.Square, accum_out=ss_h[:, b, kind, h:h + 1]).then_inc(sq_done, 1)

            def exps(j):
                S = P * (JOBS[j][2] + 1)
                act.wait_ge(logit_done, j + 1)
                for hh in range(2):
                    part = logit[j % 2][:, hh * S:hh * S + S]
                    ins = nc.scalar.activation(part, part, ACT.Exp, bias=j_nmax[:, 2 * j + hh:2 * j + hh + 1],
                                               accum_out=j_sum[:, 2 * j + hh:2 * j + hh + 1])
                ins.then_inc(exp_done, 1)

            def probT_out(j):
                S = P * (JOBS[j][2] + 1)
                act.wait_ge(pT_mm, j + 1)
                if j >= 2:
                    act.wait_ge(y_mm, j - 1)
                nc.scalar.activation(probT[j % 2][:, 0:2 * S], ps[:, 6, 0:2 * S], ACT.Copy).then_inc(pT_done, 1)

            def y_out(j):
                g, pr, b = JOBS[j]
                act.wait_ge(y_mm, j + 1)
                t = slice(b * P, b * P + P)
                dst = hT_hi[:, NH + 2 * pr:NH + 2 * pr + 2, t] if g else y_first[:, 2 * pr:2 * pr + 2, t]
                nc.scalar.activation(dst, ps[:, 7, 0:256].rearrange("p (h t) -> p h t", h=2), ACT.Copy).then_inc(yhi_done, 1)

            act.wait_ge(gain_in, 16)
            for k in range(2):
                norm_hi(0, G_ATTN, k)
            for u in range(16):
                split_hi(u, u)
                for k in range(2 * u + 2, min(2 * u + 4, KD)):
                    norm_hi(0, G_ATTN, k)
                if 4 <= u < 4 + NX * TT:
                    norm_square(0, xs, xn, u % TT, (u - 4) // TT)
                if u == 12:
                    act.wait_ge(const_in, 32)
                    norm_root(0)
                if u == 13:
                    act.wait_ge(rs_ready, 1)
                    proj_out(0)
            for s in range(SLOTS):
                split_hi(16 + s, s, width(W_IN_ORDER[s // 8 + 2]) if s < 8 * (N_IN - 2) else PIECE)
                if s in FIRST_AT:
                    for k in range(2 * FIRST_AT.index(s), 2 * FIRST_AT.index(s) + 2):
                        act.wait_ge(piece_used, 16 * (N_IN - 1) + k + 1)
                        nc.scalar.activation(hT_hi[:, k, :], y_first[:, k, :], ACT.Copy).then_inc(first_hi, 1)
                if s % 8 == 1 and s < 8 * (N_IN - 1):
                    proj_out(s // 8 + 1)
                if s == 1:
                    act.wait_ge(proj_done, 2)
                    act.wait_ge(vec_ready, 1)
                    squares = []
                    for b in range(TT):
                        squares.append(nc.scalar.activation(ps[:, 4 + 2 * b, :], proj[b][:, O_CQ:O_CQ + QL], ACT.Square, accum_out=ss_c[:, b:b + 1]))
                        squares.append(nc.scalar.activation(ps[:, 5 + 2 * b, 0:CKV], proj[b][:, O_CKV:O_CKV + CKV], ACT.Square, accum_out=ss_c[:, 2 + b:3 + b]))
                        squares.append(nc.scalar.activation(junk[:, ROPE * b:ROPE * b + ROPE], proj[b][:, O_KR:O_KR + ROPE], ACT.Square, accum_out=ss_kr[:, b:b + 1]))
                    link(*squares)
                    nc.scalar.activation(rs_c[:, 0:2], ss_c[:, 0:2], ACT.Sqrt, bias=eps[:, :], scale=1.0 / QL).then_inc(c_root, 1)
                    nc.scalar.activation(rs_c[:, 2:4], ss_c[:, 2:4], ACT.Sqrt, bias=eps[:, :], scale=1.0 / CKV).then_inc(c_root, 1)
                for k in LATENT_T.get(s - 1, ()):
                    dst, gain = (cqT[:, k, :], G_CQ + k) if k < 4 else (ckvT[:, k - 4, :], G_CKV + k - 4)
                    side_out(k, dst, ps[:, side_bank(k), 0:SEQ], scale=gains[:, gain:gain + 1])
                if 0 <= s - 1 - UP_AT < 14:
                    g = s - 1 - UP_AT
                    b, n = g // 7, g % 7
                    dst = qm[b][:, n * 512:n * 512 + 512] if n < 3 else kv[b][:, (n - 3) * 512:(n - 3) * 512 + 512]
                    side_out(SIDE_UP + g, dst, ps[:, side_bank(SIDE_UP + g), :])
                if s in SQ_FIRST:
                    b, kind, h0 = SQ_FIRST[s]
                    act.wait_ge(side_done, SIDE_UP + 7 * b + (3, 7)[kind])
                    for h in range(h0, h0 + 4):
                        sum_squares(b, kind, h)
                for b in range(TT):
                    if s == ROOT_AT[b] + 1:
                        act.wait_ge(ss_done, b + 1)
                        nc.scalar.activation(rs_h[:, b, 0:2, :], ss_h[:, b, 0:2, :], ACT.Sqrt, bias=eps[:, :], scale=1.0 / QK).then_inc(h_root, 1)
                for x, (at, srcs, dst, gain) in enumerate(groups):
                    if at == s - 1:
                        side = SIDE_T + x if x < N_EARLY else SIDE_T2 + x - N_EARLY
                        side_out(side, dst, ps[:, side_bank(side), 0:128 * len(srcs)].rearrange("p (h t) -> p h t", t=P),
                                 scale=1.0 if gain is None else gains[:, gain:gain + 1])
                for c in range(2 * (s - 1 - DOTS_AT), 2 * (s - 1 - DOTS_AT) + 2):
                    if 0 <= c < DOTS:
                        S = P * (c // (IH // 2) + 1)
                        if c >= 2:
                            act.wait_ge(acc_done, c - 1)
                        side_out(SIDE_DOT + c, relu_buf[c % 2][:, 0:2 * S], ps[:, side_bank(SIDE_DOT + c), 0:2 * S], ACT.Relu, ID ** -0.5)
                if s in SQ_NEEDED:
                    act.wait_ge(proj_done, SQ_NEEDED[s])
                for b, kind, h in SQ_SECOND.get(s, ()):
                    sum_squares(b, kind, h)
                if s == ROOT2_AT:
                    act.wait_ge(sq_done, 64)
                    nc.scalar.activation(rs_h[:, :, 2:4, :], ss_h[:, :, 2:4, :], ACT.Sqrt, bias=eps[:, :], scale=1.0 / HD).then_inc(h_root, 1)
                for j, at in enumerate(JOB_AT):
                    if s == at + 2:
                        exps(j)
                for j, at in enumerate(JOB_AT):
                    if s == at + 3:
                        probT_out(j)
                for j, at in enumerate(JOB_AT):
                    if s == at + 4:
                        y_out(j)

            for i in range(4):
                for j in range(4):
                    split_hi(B_WO + 16 + 4 * i + j, j)
                if i:
                    for b in range(TT):
                        norm_square(1, x2, x2n, b, i - 1)
            split_hi(B_PQ, 0)
            nc.scalar.activation(table_warm, eps[:, :], ACT.Sqrt)
            split_hi(B_PQ + 1, 1)
            for b in range(TT):
                norm_square(1, x2, x2n, b, NX - 1)
            norm_root(1)
            for k in range(KD):
                norm_hi(1, G_FFN, k)

            def chunk_pair(i, base, out):
                for j in range(4):
                    split_hi(i * 4 + (base + j), j)
                    if j == 1 and not (isinstance(i, int) and i == 0):
                        out(i * 2 - 1, 1)
                    if j == 3:
                        out(i * 2, 0)

            def queries_out(c, par):
                act.wait_ge(piece_used, c * 4 + (2 * B_PQ + 4))
                nc.scalar.activation(acts[:, ds(c * SEQ + A_QR, SEQ)], ps[:, par, 0:SEQ], ACT.Copy).then_inc(qr_done, 1)

            for j in range(2, 4):
                split_hi(B_PQ + j, j)
            queries_out(0, 0)
            with act.Fori(1, U_PQ // 4) as i:
                chunk_pair(i, B_PQ, queries_out)
            queries_out(15, 1)
            split_hi(B_U, 0)
            for g in range(8):
                q, b = g // TT, g % TT
                act.wait_ge(score_mm, g + 1)
                nc.scalar.activation(score[b][:, 4 * q:4 * q + 4, :], ps[:, 2 + g % 4, :].rearrange("p (c n) -> p c n", c=4), ACT.Copy).then_inc(score_done, 1)
            act.wait_ge(x2_stored, 16)

            def gelu(c, par):
                act.wait_ge(piece_used, c * 4 + (2 * B_U + 4))
                nc.scalar.activation(acts[:, ds(c * SEQ, SEQ)], ps[:, par, 0:SEQ], ACT.Gelu).then_inc(gelu_done, 1)
            for j in range(1, 4):
                split_hi(B_U + j, j)
            gelu(0, 0)
            with act.Fori(1, NKEY // 4) as i:
                chunk_pair(i, B_U, gelu)
            def gelu_beside(c, par):
                act.wait_ge(piece_used, c * 4 + (2 * B_U + 4))
                if not (isinstance(c, int) and c < NKEY // 2 + 2):
                    act.wait_ge(applied, c - (NKEY // 2 + 1))
                nc.scalar.activation(gelu_buf[par], ps[:, par, 0:SEQ], ACT.Gelu).then_inc(gelu_done, 1)

            def second_half(i, first):
                for j in range(4):
                    split_hi(i * 4 + (B_U + j), j)
                    if j == 0 and first:
                        gelu(NKEY // 2 - 1, 1)
                        act.wait_ge(slot_ready, 2 * NH)
                        nc.scalar.activation(slot[:, 2, :], slot[:, 2, :], ACT.Exp).then_inc(cexp_done, 1)
                    if j == 1 and not first:
                        gelu_beside(i * 2 - 1, 1)
                    if j == 3:
                        gelu_beside(i * 2, 0)
            second_half(NKEY // 4, True)
            second_half(NKEY // 4 + 1, False)
            with act.Fori(NKEY // 4 + 2, NKEY // 2) as i:
                second_half(i, False)

            def expert_hi(i, c):
                nc.scalar.activation(ehi[c][:, :], acts[:, ds(i * (2 * SEQ) + c * SEQ, SEQ)], ACT.Copy).then_inc(ehi_done, 1)

            def expert_pair(i):
                for j in range(4):
                    if j % 2 == 0:
                        act.wait_ge(piece_used, i * 8 + (2 * B_V + 2 * j - 4))
                        expert_hi(i, j // 2)
                    split_hi(i * 4 + (B_V + j), j)
            split_hi(B_V, 0)
            act.wait_ge(gated, SEQ // 4)
            expert_hi(0, 0)
            gelu_beside(NKEY - 1, 1)
            split_hi(B_V + 1, 1)
            expert_hi(0, 1)
            split_hi(B_V + 2, 2)
            split_hi(B_V + 3, 3)
            act.wait_ge(applied, NKEY // 2)
            with act.Fori(1, NKEY // 2) as i:
                expert_pair(i)

        @block.vector
        def _(dve):
            links = [0]
            V = nc.vector

            def link(*ins):
                for i in ins:
                    i.then_inc(dve_chain, 1)
                links[0] += len(ins)
                dve.wait_ge(dve_chain, links[0])

            def split_lo(u, j, w=PIECE):
                for half in range(2):
                    dve.wait_ge(hi_done, u * 2 + (half + 1))
                    slot_no = (2 * j + half) % NPART
                    V.tensor_tensor(wlo[slot_no][:, 0:w], raw[j % NRAW][:, half * w:half * w + w], whi[slot_no][:, 0:w].bitcast(F32),
                                    ALU.subtract).then_inc(lo_done, 1)

            def norm_sum(nth):
                dve.wait_ge(x_sq, 2 * NX * (nth + 1))
                V.tensor_reduce(ss_x, ss_part, AX, ALU.add).then_inc(x_sum, 1)

            def norm_reciprocal(nth):
                dve.wait_ge(x_root, nth + 1)
                V.reciprocal(rs_x, rs_x).then_inc(rs_ready, 1)

            def norm_lo(nth, gain, k):
                dve.wait_ge(hThi_done, nth * KD + k + 1)
                V.scalar_tensor_tensor(hT_lo[:, k, :], norm_chunk(nth, k), gains[:, gain + k:gain + k + 1],
                                       hT_hi[:, k, :].bitcast(F32), ALU.mult, ALU.subtract).then_inc(hTlo_done, 1)

            link(V.memset(kpad, 0.0))
            for k in range(2):
                norm_lo(0, G_ATTN, k)
            for u in range(16):
                split_lo(u, u)
                for k in range(2 * u + 2, min(2 * u + 4, KD)):
                    norm_lo(0, G_ATTN, k)
                if u == 9:
                    dve.wait_ge(vec_mm, 1)
                    V.tensor_copy(acts[0:8, A_VEC:A_VEC + 512], ps[0:8, 7, :]).then_inc(vec_ready, 1)
                if u == 11:
                    norm_sum(0)
                if u == 12:
                    norm_reciprocal(0)

            def per_head(b, kind, n):
                return rs_h[:, b, kind, :].unsqueeze(2).to_broadcast([P, NH, n])
            tmp = [rope_tmp[i].rearrange("p (h c) -> p h c", h=NH) for i in range(4)]
            half = ROPE // 2
            TURNS = ((0, 0), (1, 1), (0, 1), (1, 0))

            def rope_products(b):
                q = qm_h[b][:, :, NOPE:QK]
                k = proj[b][:, O_KR:O_KR + ROPE]
                link(V.tensor_tensor(q, q, rope_gain[:, 0, :].unsqueeze(1).to_broadcast([P, NH, ROPE]), ALU.mult),
                     V.tensor_tensor(k, k, rope_gain[:, 1, :], ALU.mult))
                link(*[V.tensor_tensor(tmp[i], q[:, :, part * half:part * half + half],
                                       rope_tab[:, f, b, :].unsqueeze(1).to_broadcast([P, NH, half]), ALU.mult) for i, (part, f) in enumerate(TURNS)])

            def rotated_queries(b):
                qp = qpad.rearrange("p (a r d) -> p a r d", r=2, d=128)
                ops = []
                for r in range(2):
                    t4 = [t.rearrange("p (a r) c -> p a r c", r=2)[:, :, r, :] for t in tmp]
                    ops.append(V.tensor_tensor(qp[:, :, r, r * ROPE:r * ROPE + half], t4[0], t4[1], ALU.subtract))
                    ops.append(V.tensor_tensor(qp[:, :, r, r * ROPE + half:r * ROPE + ROPE], t4[2], t4[3], ALU.add))
                link(*ops)

            def rotated_keys(b):
                k, kt, rot = proj[b][:, O_KR:O_KR + ROPE], rope_tmp[0], rope_tmp[4]
                link(*[V.tensor_tensor(kt[:, i * half:i * half + half], k[:, part * half:part * half + half], rope_tab[:, f, b, :], ALU.mult)
                       for i, (part, f) in enumerate(TURNS)])
                link(V.tensor_tensor(rot[:, 0:half], kt[:, 0:half], kt[:, half:2 * half], ALU.subtract),
                     V.tensor_tensor(rot[:, half:ROPE], kt[:, 2 * half:3 * half], kt[:, 3 * half:4 * half], ALU.add))
                V.tensor_tensor(krot.rearrange("p (h d) -> p h d", h=NH), rot.unsqueeze(1).to_broadcast([P, NH, ROPE]), per_head(b, 1, ROPE), ALU.mult).then_inc(tok_ready, 1)

            def score_keys(c):
                b, pr = c // (IH // 2), c % (IH // 2)
                S = P * (b + 1)
                acc = work[b][:, 0:S]
                dve.wait_ge(side_done, SIDE_DOT + c + 1)
                for r in range(2):
                    h = 2 * pr + r
                    w = proj[b][:, O_WI + h:O_WI + h + 1]
                    dot = relu_buf[c % 2][:, r * S:r * S + S]
                    if h:
                        ins = V.scalar_tensor_tensor(acc, dot, w, acc, ALU.mult, ALU.add)
                    else:
                        ins = V.tensor_scalar(acc, dot, w, None, ALU.mult)
                    if r:
                        ins.then_inc(acc_done, 1)
                        dve.wait_ge(acc_done, c + 1)
                    else:
                        link(ins)

            def select(b, rounds):
                left = work[b][:, 0:P * (b + 1)]
                for _ in range(rounds):
                    link(V.max(top8, left))
                    link(V.match_replace(left, top8, left, REMOVED))

            def logits(j):
                g, pr, b = JOBS[j]
                S = P * (b + 1)
                dve.wait_ge(logit_mm, j + 1)
                if j >= 2:
                    dve.wait_ge(pT_mm, j - 1)
                ops = []
                for hh in range(2):
                    h = 2 * pr + hh
                    add = bias[b][:, h, 0:S] if g else chunk_mask[:, b, 0:S]
                    ops.append(V.scalar_tensor_tensor(logit[j % 2][:, hh * S:hh * S + S], ps[:, 4 + j % 2, hh * S:hh * S + S],
                                                      rs_h[:, b, 2 * g, h:h + 1], add, ALU.mult, ALU.add))
                link(*ops)
                V.tensor_reduce(j_nmax[:, 2 * j:2 * j + 2], logit[j % 2][:, 0:2 * S].rearrange("p (h s) -> p h s", h=2), AX, ALU.max, negate=True).then_inc(logit_done, 1)

            def normalise(j):
                S = P * (JOBS[j][2] + 1)
                dve.wait_ge(exp_done, j + 1)
                link(V.reciprocal(j_rec[:, 2 * j:2 * j + 2], j_sum[:, 2 * j:2 * j + 2]))
                for hh in range(2):
                    part = logit[j % 2][:, hh * S:hh * S + S]
                    ins = V.tensor_scalar(part, part, j_rec[:, 2 * j + hh:2 * j + hh + 1], None, ALU.mult)
                ins.then_inc(prob_done, 1)

            def y_lo(j):
                g, pr, b = JOBS[j]
                k = NH + 2 * pr
                dve.wait_ge(yhi_done, j + 1)
                V.tensor_tensor(hT_lo[:, k:k + 2, b * P:b * P + P], ps[:, 7, 0:256].rearrange("p (h t) -> p h t", h=2),
                                hT_hi[:, k:k + 2, b * P:b * P + P].bitcast(F32), ALU.subtract).then_inc(ylo_done, 1)

            def residual(i):
                n = i % 4
                if i == 0:
                    dve.wait_ge(x_back, 16)
                elif i >= 4:
                    dve.wait_ge(x2_done, 2 * (n + 1))
                dve.wait_ge(piece_used, 2 * B_WO + 8 * i + 8)
                for b in range(TT):
                    cols = x2[b][:, n * 512:n * 512 + 512]
                    V.tensor_tensor(cols, ps[:, 2 * (i % 2) + b, :], cols, ALU.add).then_inc(x2_done, 1)

            for s in range(SLOTS):
                split_lo(16 + s, s, width(W_IN_ORDER[s // 8 + 2]) if s < 8 * (N_IN - 2) else PIECE)
                if s in FIRST_AT:
                    for k in range(2 * FIRST_AT.index(s), 2 * FIRST_AT.index(s) + 2):
                        dve.wait_ge(first_hi, k + 1)
                        V.tensor_tensor(hT_lo[:, k, :], y_first[:, k, :], hT_hi[:, k, :].bitcast(F32), ALU.subtract).then_inc(first_lo, 1)
                if s == 2:
                    dve.wait_ge(c_root, 2)
                    link(V.reciprocal(rs_c, rs_c))
                    for b in range(TT):
                        V.tensor_scalar(proj[b][:, O_CQ:O_CQ + QL], proj[b][:, O_CQ:O_CQ + QL], rs_c[:, b:b + 1], None, ALU.mult).then_inc(cn_done, 1)
                        V.tensor_scalar(proj[b][:, O_CKV:O_CKV + CKV], proj[b][:, O_CKV:O_CKV + CKV], rs_c[:, 2 + b:3 + b], None, ALU.mult).then_inc(cn_done, 1)
                if s == 4:
                    dve.wait_ge(mask_in, 64)
                for b in range(TT):
                    if s == ROOT_AT[b]:
                        dve.wait_ge(sq_done, 16 * (b + 1))
                        V.tensor_scalar(ss_h[:, b, 1, :], ss_h[:, b, 1, :], ss_kr[:, b:b + 1], None, ALU.add).then_inc(ss_done, 1)
                    if s == ROOT_AT[b] + 1:
                        dve.wait_ge(h_root, b + 1)
                        link(V.reciprocal(rs_h[:, b, 0:2, :], rs_h[:, b, 0:2, :]))
                        link(V.tensor_scalar(rs_h[:, b, 0, :], rs_h[:, b, 0, :], QK ** -0.5, None, ALU.mult))
                        kn = kv_h[b][:, :, 0:NOPE]
                        V.tensor_tensor(kn, kn, per_head(b, 1, NOPE), ALU.mult).then_inc(tok_ready, 1)
                    if s == ROPE_AT[b]:
                        rope_products(b)
                    if s == QPAD_AT[b]:
                        if b == 0:
                            dve.wait_ge(side_mm, SIDE_UP + 14)
                            link(V.memset(qpad, 0.0))
                        else:
                            dve.wait_ge(side_mm, SIDE_T + 5)
                        rotated_queries(b)
                    if s == KROT_AT[b]:
                        rotated_keys(b)
                    if s == KPAD_AT[b]:
                        dve.wait_ge(proj_done, 5)
                        if b:
                            dve.wait_ge(side_mm, SIDE_T + 17)
                        key = proj[b][:, O_KI:O_KI + ID]
                        V.tensor_copy(kpad[:, 0, 0:ID], key)
                        V.tensor_copy(kpad[:, 1, ID:2 * ID], key).then_inc(tok_ready, 1)
                for c in range(2 * (s - 1 - DOTS_AT), 2 * (s - 1 - DOTS_AT) + 2):
                    if 0 <= c < DOTS:
                        score_keys(c)
                turn = s - SELECT_AT
                if 0 <= turn < 4 * TT:
                    b = turn // 4
                    left = work[b][:, 0:P * (b + 1)]
                    if turn % 4 == 0:
                        link(V.tensor_tensor(left, left, chunk_mask[:, b, 0:P * (b + 1)], ALU.add))
                    select(b, N_SEL // 32)
                if 0 <= turn - 4 * TT < TT:
                    b = turn - 4 * TT
                    S = P * (b + 1)
                    left = work[b][:, 0:S]
                    dve.wait_ge(bias_in, 32)
                    link(V.tensor_scalar(left, left, REMOVED / 2, MASKED, ALU.is_gt, ALU.mult))
                    link(V.tensor_tensor(bias[b][:, :, 0:S], bias[b][:, :, 0:S], left.unsqueeze(1).to_broadcast([P, NH, S]), ALU.add))
                if s == ROOT2_AT:
                    dve.wait_ge(h_root, 3)
                    link(V.reciprocal(rs_h[:, :, 2:4, :], rs_h[:, :, 2:4, :]))
                    link(V.tensor_scalar(rs_h[:, :, 2, :], rs_h[:, :, 2, :], HD ** -0.5, None, ALU.mult))
                if s in (ROOT2_AT, ROOT2_AT + 1):
                    b = s - ROOT2_AT
                    kd = proj[b][:, O_KD:O_VD].rearrange("p (h d) -> p h d", h=NH)
                    V.tensor_tensor(kd, kd, per_head(b, 3, HD), ALU.mult).then_inc(tok_ready, 1)
                for j, at in enumerate(JOB_AT):
                    if s == at + 1:
                        logits(j)
                for j, at in enumerate(JOB_AT):
                    if s == at + 2:
                        normalise(j)
                for j, at in enumerate(JOB_AT):
                    if s == at + 4 and JOBS[j][0]:
                        y_lo(j)
                if s >= 69 and (s - 69) % 4 == 0:
                    residual((s - 69) // 4)
            for i in range(4):
                for j in range(4):
                    split_lo(B_WO + 16 + 4 * i + j, j)
                    if j == 1:
                        residual(3 + i)
            split_lo(B_PQ, 0)
            residual(7)
            split_lo(B_PQ + 1, 1)

            norm_sum(1)
            norm_reciprocal(1)
            dve.wait_ge(rs_ready, 2)
            for b in range(TT):
                V.tensor_scalar(diag[b], ident[:, :], rs_x[:, b:b + 1], None, ALU.mult).then_inc(diag_done, 1)
            for k in range(KD):
                norm_lo(1, G_FFN, k)
            for j in range(2, 4):
                split_lo(B_PQ + j, j)
            with dve.Fori(1, U_PQ // 4) as i:
                for j in range(4):
                    split_lo(i * 4 + (B_PQ + j), j)

            steps = 15
            with dve.Fori(0, TT * NH) as i:
                count = [0]

                def step(*ins):
                    ins[-1].then_inc(head_step, 1)
                    count[0] += 1
                    dve.wait_ge(head_step, i * steps + count[0])
                    V.memset(carrier, 0.0)

                def split(j):
                    split_lo(i * 8 + (B_U + j), j)
                halves = [h_score[:, f, :] for f in range(2)]
                split(0)
                dve.wait_ge(score_done, 8)
                step(V.tensor_copy(h_score, acts[:, ds(i * 256 + A_SCORE, 256)].rearrange("p (f n) -> p f n", f=2)))
                step(*[V.max(top_v[:, f, 0:8], halves[f]) for f in range(2)])
                split(1)
                step(*[V.max_index(top_iu[:, f, 0:8], top_v[:, f, 0:8], halves[f]) for f in range(2)],
                     *[V.match_replace(halves[f], top_v[:, f, 0:8], halves[f], REMOVED) for f in range(2)])
                step(*[V.max(top_v[:, f, 8:16], halves[f]) for f in range(2)])
                split(2)
                step(*[V.max_index(top_iu[:, f, 8:16], top_v[:, f, 8:16], halves[f]) for f in range(2)])
                step(V.tensor_copy(top_i, top_iu),
                     V.tensor_tensor(cand.rearrange("p (i j) -> p i j", i=TOPK), top_v[:, 0, :].unsqueeze(2).to_broadcast([P, TOPK, TOPK]),
                                     top_v[:, 1, :].unsqueeze(1).to_broadcast([P, TOPK, TOPK]), ALU.add))
                split(3)
                step(V.max(c_v[:, 0:8], cand))
                step(V.max_index(c_iu[:, 0:8], c_v[:, 0:8], cand), V.match_replace(cand, c_v[:, 0:8], cand, REMOVED))
                split(4)
                step(V.max(c_v[:, 8:16], cand))
                step(V.max_index(c_iu[:, 8:16], c_v[:, 8:16], cand))
                split(5)
                step(V.tensor_scalar(c_digit_u[:, 0, :], c_iu, 4, None, ALU.logical_shift_right),
                     V.tensor_scalar(c_digit_u[:, 1, :], c_iu, 15, None, ALU.bitwise_and))
                step(V.tensor_copy(c_digit, c_digit_u))
                split(6)
                step(V.tensor_tensor(pick, c_digit.unsqueeze(3).to_broadcast([P, 2, TOPK, TOPK]),
                                     iota[:, 0:TOPK].unsqueeze(1).unsqueeze(1).to_broadcast([P, 2, TOPK, TOPK]), ALU.is_equal))
                step(V.tensor_tensor(pick, pick, top_i.unsqueeze(2).to_broadcast([P, 2, TOPK, TOPK]), ALU.mult))
                split(7)
                for f in range(2):
                    V.tensor_reduce(acts[:, ds(i * TOPK + (A_SLOT + f * SEQ), TOPK)], pick[:, f], AX, ALU.add)
                V.tensor_scalar(acts[:, ds(i * TOPK + (A_SLOT + 2 * SEQ), TOPK)], c_v, c_v[:, 0:1], None, ALU.subtract).then_inc(slot_ready, 1)
                step(V.tensor_copy(top8, c_v[:, 0:8]))
                assert count[0] == steps

            slotT_flat = slotT[:, :, :].rearrange("p f t -> p (f t)")

            def hots(g):
                for k in range(4):
                    if not (isinstance(g, int) and g == 0):
                        dve.wait_ge(gate_mm, g * 4 + (k - 3))
                    V.tensor_scalar(hot1[k], iota[:, :], slotT_flat[:, ds(g * 4 + (k + SEQ), 1)], None, ALU.is_equal)
                    V.tensor_scalar(hot0[k], iota[:, :], slotT_flat[:, ds(g * 4 + k, 1)], slotT_flat[:, ds(g * 4 + (k + 2 * SEQ), 1)],
                                    ALU.is_equal, ALU.mult).then_inc(hot_done, 1)

            def gate(g, par):
                dve.wait_ge(gate_mm, g * 4 + 4)
                a = acts_e[:, :, ds(g * 4, 4)].rearrange("p e t -> p t e")
                V.tensor_tensor(a, a, ps[:, 2 + par, :].rearrange("p (t e) -> p t e", t=4), ALU.mult).then_inc(gated, 1)

            def apply(c, par, groups):
                dve.wait_ge(gelu_done, c + 1)
                dve.wait_ge(gated, groups)
                col = acts[:, ds(c * SEQ, SEQ)]
                V.tensor_tensor(col, col, gelu_buf[par], ALU.mult).then_inc(applied, 1)

            def second_half(i):
                g = i * 2 - NKEY // 2
                split_lo(i * 4 + B_U, 0)
                hots(g)
                split_lo(i * 4 + (B_U + 1), 1)
                dve.wait_ge(applied, g - 1)
                gate(g - 1, 1)
                apply(i * 2 - 1, 1, g)
                split_lo(i * 4 + (B_U + 2), 2)
                hots(g + 1)
                split_lo(i * 4 + (B_U + 3), 3)
                dve.wait_ge(applied, g)
                gate(g, 0)
                apply(i * 2, 0, g + 1)
            first = NKEY // 4
            split_lo(4 * first + B_U, 0)
            dve.wait_ge(cexp_done, 1)
            gates = slot[:, 2, :].rearrange("p (h j) -> p h j", j=TOPK)
            link(V.tensor_reduce(gate_sum[:, 0, :], gates, AX, ALU.add))
            link(V.reciprocal(gate_sum[:, 1, :], gate_sum[:, 0, :]))
            V.tensor_tensor(gates, gates, gate_sum[:, 1, :].unsqueeze(2).to_broadcast([P, TT * NH, TOPK]), ALU.mult).then_inc(slot_done, 1)
            split_lo(4 * first + (B_U + 1), 1)
            split_lo(4 * first + (B_U + 2), 2)
            for b in range(TT):
                dve.wait_ge(slotT_mm, b + 1)
                V.tensor_copy(slotT[:, :, b * P:b * P + P], ps[:, 6 + b, 0:384].rearrange("p (f t) -> p f t", f=3)).then_inc(slotT_done, 1)
            dve.wait_ge(slotT_done, TT)
            split_lo(4 * first + (B_U + 3), 3)
            hots(0)
            hots(1)
            dve.wait_ge(ones_set, 4)
            gate(0, 0)
            apply(NKEY // 2, 0, 1)
            with dve.Fori(NKEY // 4 + 1, NKEY // 2) as i:
                second_half(i)
            dve.wait_ge(applied, NKEY // 2 - 1)
            gate(SEQ // 4 - 1, 1)

            def expert_lo(i, c):
                dve.wait_ge(ehi_done, i * 2 + (c + 1))
                V.tensor_tensor(elo[c][:, :], acts[:, ds(i * (2 * SEQ) + c * SEQ, SEQ)], ehi[c][:, :].bitcast(F32),
                                ALU.subtract).then_inc(elo_done, 1)

            def expert_pair(i):
                for j in range(4):
                    if j % 2 == 0:
                        expert_lo(i, j // 2)
                    split_lo(i * 4 + (B_V + j), j)
            split_lo(B_V, 0)
            dve.wait_ge(gated, SEQ // 4)
            expert_lo(0, 0)
            apply(NKEY - 1, 1, SEQ // 4)
            split_lo(B_V + 1, 1)
            expert_lo(0, 1)
            split_lo(B_V + 2, 2)
            split_lo(B_V + 3, 3)
            dve.wait_ge(applied, NKEY // 2)
            with dve.Fori(1, NKEY // 2) as i:
                expert_pair(i)
            dve.wait_ge(x2_back, 16)
            for g in range(8):
                n, b = g // TT, g % TT
                dve.wait_ge(piece_used, 2 * B_END - 3 + n)
                V.tensor_tensor(xn[b][:, n * 512:n * 512 + 512], ps[:, 4 * b + n, :], xs[b][:, n * 512:n * 512 + 512], ALU.add).then_inc(out_ready, 1)

        @block.tensor
        def _(pe):
            mm = nc.tensor.matmul

            def norm_transpose(k):
                if k >= NT:
                    pe.wait_ge(hTlo_done, KD + k + 1 - NT)
                for b in range(TT):
                    ins = mm(ps[:, norm_bank(k), b * P:b * P + P], x2[b][:, k * P:k * P + P], diag[b], start=True, stop=True)
                ins.then_inc(xT_mm, 1)

            def tall_unit(u, j, k0, par, w, start, stop):
                for kk in range(2):
                    k, part = k0 + kk, (2 * j + kk) % NPART
                    pe.wait_ge(lo_done, u * 2 + (kk + 1))
                    for b in range(TT):
                        out = ps[:, 2 * par + b, 0:w]
                        t = slice(b * P, b * P + P)
                        mm(out, hT_hi[:, k, t], whi[part][:, 0:w], start=start and kk == 0, stop=False)
                        mm(out, hT_hi[:, k, t], wlo[part][:, 0:w], start=False, stop=False)
                        ins = mm(out, hT_lo[:, k, t], whi[part][:, 0:w], start=False, stop=stop and kk == 1)
                    ins.then_inc(piece_used, 1)

            def side_turn(x):
                if x >= 4:
                    pe.wait_ge(side_done, x - 3)
                return side_bank(x)

            def up_projection(g):
                b, n = g // 7, g % 7
                bank = side_turn(SIDE_UP + g)
                if g == 0:
                    pe.wait_ge(wu_in, 96)
                if n in (0, 3):
                    pe.wait_ge(side_done, SIDE_UP)
                src, w, ks = (cqT, w_uq[:, :, n * 512:n * 512 + 512], 4) if n < 3 else (ckvT, w_ukv[:, :, (n - 3) * 512:(n - 3) * 512 + 512], 2)
                for k in range(ks):
                    ins = mm(ps[:, bank, :], src[:, k, b * P:b * P + P], w[:, k, :], start=k == 0, stop=k == ks - 1)
                ins.then_inc(side_mm, 1)

            def indexer_dots(c):
                b, pr = c // (IH // 2), c % (IH // 2)
                S = P * (b + 1)
                bank = side_turn(SIDE_DOT + c)
                if c == 0:
                    pe.wait_ge(side_done, SIDE_DOT)
                for r in range(2):
                    ins = mm(ps[:, bank, r * S:r * S + S], qiT[:, pr, b * P:b * P + P], kiT[:, r, 0:S], start=True, stop=True)
                ins.then_inc(side_mm, 1)

            def products(j):
                g, pr, b = JOBS[j]
                S = P * (b + 1)
                t = slice(b * P, b * P + P)
                if j in (0, 8):
                    pe.wait_ge(side_done, SIDE_END if j else SIDE_T2)
                else:
                    pe.wait_ge(logit_done, max(j - 1, 1))
                for hh in range(2):
                    h = 2 * pr + hh
                    out = ps[:, 4 + j % 2, hh * S:hh * S + S]
                    if g == 0:
                        mm(out, qTn[:, h, t], kTn[:, h, 0:S], start=True, stop=False)
                        ins = mm(out, qTr[:, h, t], kTr[:, pr, 0:S], start=False, stop=True)
                    else:
                        ins = mm(out, qdT[:, h, t], kdT[:, h, 0:S], start=True, stop=True)
                ins.then_inc(logit_mm, 1)

            def prob_transpose(j):
                pe.wait_ge(prob_done, j + 1)
                if j:
                    pe.wait_ge(pT_done, j)
                for i in range(2 * (JOBS[j][2] + 1)):
                    ins = nc.tensor.transpose(ps[:, 6, i * P:i * P + P], logit[j % 2][:, i * P:i * P + P], ident[:, :])
                ins.then_inc(pT_mm, 1)

            def values(j):
                g, pr, b = JOBS[j]
                pe.wait_ge(pT_done, j + 1)
                if j:
                    pe.wait_ge(yhi_done, j)
                if j > 8:
                    pe.wait_ge(ylo_done, j - 8)
                if j == 8:
                    pe.wait_ge(proj_done, N_IN)
                for hh in range(2):
                    h = 2 * pr + hh
                    for s in range(b + 1):
                        v = proj[s][:, O_VD + h * HD:O_VD + h * HD + HD] if g else kv_h[s][:, h, NOPE:NOPE + HD]
                        i = hh * (b + 1) + s
                        ins = mm(ps[:, 7, hh * P:hh * P + P], v, probT[j % 2][:, i * P:i * P + P], start=s == 0, stop=s == b)
                ins.then_inc(y_mm, 1)

            for j in range(8):
                pe.wait_ge(hTlo_done, 2 * j + 2)
                tall_unit(j, j, 2 * j, 0, 512, j == 0, j == 7)
            pe.wait_ge(hot_in, 32)
            mm(ps[0:8, 7, :], acts[0:32, A_BIAS + 512:A_BIAS + 520], acts[0:32, A_BIAS:A_BIAS + 512], start=True, stop=True).then_inc(vec_mm, 1)
            for j in range(8):
                tall_unit(8 + j, j, 2 * j, 1, 512, j == 0, j == 7)
            pe.wait_ge(const_in, 32)
            for s in range(SLOTS):
                if s < 8 * (N_IN - 2):
                    pos, j = s // 8 + 2, s % 8
                    if j == 0:
                        pe.wait_ge(proj_done, pos - 1)
                    tall_unit(16 + s, j, 2 * j, pos % 2, width(W_IN_ORDER[pos]), j == 0, j == 7)
                else:
                    i, j = (s - 8 * (N_IN - 2)) // 4, s % 4
                    if j == 0 and i < 2:
                        pe.wait_ge(proj_done, N_IN - 1 + i)
                    elif j == 0:
                        pe.wait_ge(x2_done, 2 * (i - 1))
                    if i == 0:
                        pe.wait_ge(first_lo, 2 * j + 2)
                    tall_unit(16 + s, j, 2 * j, i % 2, 512, j == 0, j == 3)
                if s == 2:
                    pe.wait_ge(cn_done, 2 * TT)
                for k in LATENT_T.get(s, ()):
                    bank = side_turn(k)
                    off = O_CQ + P * k if k < 4 else O_CKV + P * (k - 4)
                    for b in range(TT):
                        ins = nc.tensor.transpose(ps[:, bank, b * P:b * P + P], proj[b][:, off:off + P], ident[:, :])
                    ins.then_inc(side_mm, 1)
                if 0 <= s - UP_AT < 14:
                    up_projection(s - UP_AT)
                for x, (at, srcs, dst, gain) in enumerate(groups):
                    if at == s:
                        side = SIDE_T + x if x < N_EARLY else SIDE_T2 + x - N_EARLY
                        if s in TOK_NEEDED:
                            pe.wait_ge(tok_ready, TOK_NEEDED[s])
                        if x == N_EARLY:
                            pe.wait_ge(yhi_done, 8)
                        bank = side_turn(side)
                        for i, src in enumerate(srcs):
                            ins = nc.tensor.transpose(ps[:, bank, i * P:i * P + P], src, ident[:, :])
                        ins.then_inc(side_mm, 1)
                for c in range(2 * (s - DOTS_AT), 2 * (s - DOTS_AT) + 2):
                    if 0 <= c < DOTS:
                        indexer_dots(c)
                for j, at in enumerate(JOB_AT):
                    if s == at:
                        products(j)
                for j, at in enumerate(JOB_AT):
                    if s == at + 2:
                        prob_transpose(j)
                for j, at in enumerate(JOB_AT):
                    if s == at + 3:
                        values(j)

            pe.wait_ge(ylo_done, 8)
            with pe.Fori(0, 2) as i:
                for par in range(2):
                    pe.wait_ge(x2_done, i * 4 + (2 * par + 6))
                    for j in range(4):
                        tall_unit(i * 8 + (B_WO + 16 + 4 * par + j), j, NH + 2 * j, par, 512, j == 0, j == 3)
            pe.wait_ge(diag_done, TT)
            for k in range(NT):
                norm_transpose(k)

            def wide_piece(i, base, j, c):
                pe.wait_ge(lo_done, i * 8 + (2 * base + j + 1))
                for kk in range(4):
                    k = 4 * (j % 4) + kk
                    w = slice(kk * P, kk * P + P)
                    out = ps[:, c, 0:SEQ]
                    mm(out, whi[j % NPART][:, w], hT_hi[:, k, :], start=k == 0, stop=False)
                    mm(out, whi[j % NPART][:, w], hT_lo[:, k, :], start=False, stop=False)
                    ins = mm(out, wlo[j % NPART][:, w], hT_hi[:, k, :], start=False, stop=k == KD - 1)
                ins.then_inc(piece_used, 1)

            def wide_pair(i, base, out_done, before=lambda piece: None):
                for c in range(2):
                    if not (isinstance(i, int) and i == 0):
                        pe.wait_ge(out_done, i * 2 + (c - 1))
                    for j in range(4):
                        before(4 * c + j)
                        wide_piece(i, base, 4 * c + j, c)

            def rest_of_norm(piece):
                for k in range(NT + 4 * piece, min(NT + 4 * piece + 4, KD)):
                    norm_transpose(k)
                if piece < 4:
                    pe.wait_ge(hTlo_done, KD + 4 * piece + 4)
            wide_pair(0, B_PQ, qr_done, rest_of_norm)
            with pe.Fori(1, U_PQ // 4) as i:
                wide_pair(i, B_PQ, qr_done)
            pe.wait_ge(subk_in, 16)
            for g in range(8):
                q, b = g // TT, g % TT
                pe.wait_ge(qr_done, 4 * q + 4)
                if g >= 4:
                    pe.wait_ge(score_done, g - 3)
                for i in range(4):
                    c = 4 * q + i
                    ins = mm(ps[:, 2 + g % 4, i * P:i * P + P], qr[:, c, b * P:b * P + P], subk[:, c, :], start=True, stop=True)
                ins.then_inc(score_mm, 1)
            wide_pair(0, B_U, gelu_done)
            with pe.Fori(1, NKEY // 4) as i:
                wide_pair(i, B_U, gelu_done)
            def gate_group(g, q, first):
                if not first:
                    pe.wait_ge(gated, g - 1)
                for k in range(4):
                    pe.wait_ge(hot_done, g * 4 + (k + 1))
                    mm(ps[:, 2 + q, k * P:k * P + P], hot1[k], hot0[k], start=True, stop=True).then_inc(gate_mm, 1)

            def slot_transposes():
                pe.wait_ge(slot_done, 1)
                for b in range(TT):
                    for f in range(3):
                        ins = nc.tensor.transpose(ps[:, 6 + b, f * P:f * P + P], slot[:, f, b * P:b * P + P], ident[:, :])
                    ins.then_inc(slotT_mm, 1)

            def second_half(i, first):
                for c in range(2):
                    pe.wait_ge(gelu_done, i * 2 + (c - 1))
                    for j in range(4):
                        wide_piece(i, B_U, 4 * c + j, c)
                        if first:
                            if 4 * c + j == 3:
                                slot_transposes()
                            if 4 * c + j >= 6:
                                gate_group(4 * c + j - 6, 4 * c + j - 6, True)
                        elif j == 2:
                            gate_group(i * 2 + (c - NKEY // 2), c, False)
            second_half(NKEY // 4, True)
            with pe.Fori(NKEY // 4 + 1, NKEY // 2) as i:
                second_half(i, False)

            pe.wait_ge(gated, SEQ // 4)

            def expert_pair(i, first, last):
                for c in range(2):
                    pe.wait_ge(elo_done, i * 2 + (c + 1))
                    for q in range(4):
                        pe.wait_ge(lo_done, i * 8 + (2 * B_V + 4 * c + q + 1))
                        if first and (c, q) == (0, 1):
                            pe.wait_ge(gelu_done, NKEY)
                        start, stop = first and c == 0, last and c == 1
                        for b in range(TT):
                            t = slice(b * P, b * P + P)
                            out = ps[:, 4 * b + q, :]
                            mm(out, ehi[c][:, t], whi[q][:, :], start=start, stop=False)
                            mm(out, ehi[c][:, t], wlo[q][:, :], start=False, stop=False)
                            ins = mm(out, elo[c][:, t], whi[q][:, :], start=False, stop=stop)
                        ins.then_inc(piece_used, 1)
            expert_pair(0, True, False)
            with pe.Fori(1, NKEY // 2 - 1) as i:
                expert_pair(i, False, False)
            expert_pair(NKEY // 2 - 1, False, True)

    return nc


def t5_bucket_of_distance(rel):
    n = np.abs(rel)
    nf = np.maximum(n, 1).astype(np.float32)
    large = 8 + (np.log(nf / np.float32(8)) / np.float32(math.log(16)) * np.float32(8)).astype(np.int32)
    return np.where(rel > 0, 16, 0) + np.where(n < 8, n, np.minimum(large, 15))


def shape_constants(seq):
    half, chunk, tiles = 32, 64, seq // 128
    pos = np.arange(seq)
    freqs = np.float32(10000.0) ** (np.float32(-2.0) * np.arange(half, dtype=np.float32) / np.float32(2 * half))
    ang = pos.astype(np.float32)[:, None] * freqs[None, :]
    rope = np.stack([np.cos(ang), np.sin(ang)]).reshape(2, tiles, 128, half).transpose(2, 0, 1, 3).reshape(128, -1)
    mask = np.where(pos[None, :] // chunk <= pos[:, None] // chunk, 0.0, -1.0e30)
    mask = mask.reshape(tiles, 128, seq).transpose(1, 0, 2).reshape(128, -1)
    distance = np.arange(512) - (seq - 1)
    hot = np.arange(32)[:, None] == t5_bucket_of_distance(distance)[None, :]
    made = {
        "ident": np.eye(128), "iota": np.tile(np.arange(128), (128, 1)), "eps": np.full((128, 1), 1e-6),
        "rope_tab": rope, "chunk_mask": mask, "bucket_hot": hot,
    }
    return {n: np.ascontiguousarray(a, dtype=np.float32) for n, a in made.items()}


def kernel(**inputs):
    import concourse.bacc as _bacc
    from concourse import mybir as _mybir
    from concourse.bass_utils import run_bass_kernel_spmd as _run

    a = {n: np.asarray(v) for n, v in inputs.items()}
    seq, d = a["x"].shape[1:]
    columns = lambda g: g.reshape(-1, 128).T
    sent = {
        "x": a["x"][0], "w_in": a["w_in"][0], "w_uq": a["w_uq"][0], "w_ukv": a["w_ukv"][0], "w_o": a["w_o"][0],
        "rel_bias": a["rel_bias"], "v_tab": a["v_tab"][0],
        "gains": np.concatenate([columns(a["g_attn"]), columns(a["g_ffn"]), columns(a["g_cq"]), columns(a["g_ckv"]),
                                 columns(a["g_mla_q"][:, 0:128]), columns(a["g_mla_k"][:, 0:128]), columns(a["g_dsa_q"]), columns(a["g_dsa_k"])], axis=1),
        "rope_gain": np.concatenate([a["g_mla_q"][:, 128:], a["g_mla_k"][:, 128:]], axis=1),
        "xT": a["x"][0].reshape(seq, -1, 128).transpose(2, 1, 0),
        "w_pq": a["w_pq"][0].reshape(2, 8, 128, 16, 128).transpose(3, 0, 2, 1, 4).reshape(-1, 1024),
        "u_tab": a["u_tab"][0].reshape(128, 128, 2, 8, 128).transpose(0, 2, 4, 3, 1).reshape(-1, 1024),
        "sub_keys": a["sub_keys"][0].reshape(16, 128, 128).transpose(2, 0, 1),
    }
    arrays = {f"in_{n}": np.ascontiguousarray(v) for n, v in {**sent, **shape_constants(seq)}.items()}
    nc = _bacc.Bacc("TRN2", target_bir_lowering=False, num_devices=1)
    f32 = _mybir.dt.float32
    io = {n[3:]: nc.dram_tensor(n, v.shape, _mybir.dt.from_np(v.dtype), kind="ExternalInput").ap() for n, v in arrays.items()}
    io["out"] = nc.dram_tensor("out_0", (seq, d), f32, kind="ExternalOutput").ap()
    io["x2_scratch"] = nc.dram_tensor("x2_scratch", (seq, d), f32, kind="Internal").ap()
    io["bias_scratch"] = nc.dram_tensor("bias_scratch", (8, 128, 512), f32, kind="Internal").ap()
    build_block(nc, io)
    r = _run(nc, [arrays], core_ids=[0])
    return r.results[0]["out_0"].reshape(1, seq, d)
```
